# Optimizing a Trainium2 kernel written in Bass

```python
import jax, jax.numpy as jnp
from jax import lax
import numpy as np

D_MODEL = 1024
BATCH = 1
SEQ = 256
DEPTH = 2

N_MEM = 256
MLA_HEADS = 4
MLA_Q_RANK = 256
MLA_KV_RANK = 128
MLA_NOPE_DIM = 64
MLA_ROPE_DIM = 32
MLA_V_DIM = 64
FOX_HEADS = 6
FOX_HEAD_DIM = 64
FOX_GATE_BIAS_MEAN = 3.0
DIL_HEADS = 6
DIL_HEAD_DIM = 64
DILATED_PAIRS = ((128, 1), (512, 4), (2048, 16))
D_MIX = MLA_HEADS * MLA_V_DIM + FOX_HEADS * FOX_HEAD_DIM + DIL_HEADS * DIL_HEAD_DIM
IN_SPLITS = (MLA_Q_RANK, MLA_KV_RANK, MLA_ROPE_DIM,
             3 * FOX_HEADS * FOX_HEAD_DIM, FOX_HEADS,
             3 * DIL_HEADS * DIL_HEAD_DIM)
IN_COLS = sum(IN_SPLITS)
XATTN_HEADS = 4
N_EXPERTS = 16
N_GROUPS = 4
EXPERTS_PER_GROUP = N_EXPERTS // N_GROUPS
TOP_K = 2
D_EXPERT = 256
ROPE_THETA = 10000.0
Q_BLOCK = 128
DIL_BLOCK = 64
NORM_EPS = 1e-5
NEG_INF = -1e30
DEEPNORM_ALPHA = (2 * DEPTH) ** 0.25
DEEPNORM_BETA = (8 * DEPTH) ** -0.25

kernel_name = "hybrid_mla_fox_dilated_moe_deepnorm"

def layer_norm(x, g, b):
    xf = x.astype(jnp.float32)
    mu = jnp.mean(xf, axis=-1, keepdims=True)
    var = jnp.mean(jnp.square(xf - mu), axis=-1, keepdims=True)
    return ((xf - mu) * lax.rsqrt(var + NORM_EPS) * g.astype(jnp.float32) + b.astype(jnp.float32)).astype(x.dtype)

def rms_norm(x, g):
    xf = x.astype(jnp.float32)
    ms = jnp.mean(jnp.square(xf), axis=-1, keepdims=True)
    return (xf * lax.rsqrt(ms + NORM_EPS) * g.astype(jnp.float32)).astype(x.dtype)

def rope(x, positions):
    half = x.shape[-1] // 2
    inv_freq = ROPE_THETA ** (-jnp.arange(half, dtype=jnp.float32) / half)
    ang = positions.astype(jnp.float32)[:, None, :, None] * inv_freq
    cos, sin = jnp.cos(ang), jnp.sin(ang)
    xf = x.astype(jnp.float32)
    x1, x2 = xf[..., :half], xf[..., half:]
    return jnp.concatenate([x1 * cos - x2 * sin, x1 * sin + x2 * cos], axis=-1).astype(x.dtype)

def to_heads(t, n_heads):
    b, s, _ = t.shape
    return t.reshape(b, s, n_heads, -1).transpose(0, 2, 1, 3)

def from_heads(t):
    b, h, s, d = t.shape
    return t.transpose(0, 2, 1, 3).reshape(b, s, h * d)

def causal_block_attention(q, k, v, log_decay=None):
    B, H, S, Dk = q.shape
    Dv = v.shape[-1]
    nb = S // Q_BLOCK
    scale = Dk ** -0.5
    kf = k.astype(jnp.float32)
    vf = v.astype(jnp.float32)
    kpos = jnp.arange(S)
    qb = q.astype(jnp.float32).reshape(B, H, nb, Q_BLOCK, Dk).transpose(2, 0, 1, 3, 4)
    xs = (jnp.arange(nb), qb)
    if log_decay is not None:
        xs = xs + (log_decay.reshape(B, H, nb, Q_BLOCK).transpose(2, 0, 1, 3),)

    def one_block(args):
        i, q_i = args[0], args[1]
        s = jnp.einsum('bhqd,bhkd->bhqk', q_i, kf) * scale
        if log_decay is not None:
            s = s + args[2][..., :, None] - log_decay[:, :, None, :]
        qpos = i * Q_BLOCK + jnp.arange(Q_BLOCK)
        s = jnp.where(kpos[None, :] <= qpos[:, None], s, NEG_INF)
        p = jax.nn.softmax(s, axis=-1)
        return jnp.einsum('bhqk,bhkd->bhqd', p, vf)

    out = lax.map(one_block, xs)
    return out.transpose(1, 2, 0, 3, 4).reshape(B, H, S, Dv).astype(v.dtype)

def dilated_mixture_attention(q, k, v):
    B, H, S, D = q.shape
    nb = S // DIL_BLOCK
    scale = D ** -0.5
    kf = k.astype(jnp.float32)
    vf = v.astype(jnp.float32)
    qb = q.astype(jnp.float32).reshape(B, H, nb, DIL_BLOCK, D).transpose(2, 0, 1, 3, 4)

    def one_block(args):
        i, q_i = args
        qpos = i * DIL_BLOCK + jnp.arange(DIL_BLOCK)
        maxes, dens, nums = [], [], []
        for window, dilation in DILATED_PAIRS:
            offs = dilation * jnp.arange(window // dilation + 1)
            idx = qpos[:, None] - offs[None, :]
            valid = idx >= 0
            idx = jnp.maximum(idx, 0)
            k_g = jnp.take(kf, idx, axis=2)
            v_g = jnp.take(vf, idx, axis=2)
            s = jnp.einsum('bhqd,bhqnd->bhqn', q_i, k_g) * scale
            s = jnp.where(valid, s, NEG_INF)
            m = jnp.max(s, axis=-1, keepdims=True)
            p = jnp.exp(s - m)
            maxes.append(m)
            dens.append(jnp.sum(p, axis=-1, keepdims=True))
            nums.append(jnp.einsum('bhqn,bhqnd->bhqd', p, v_g))
        m_all = jnp.stack(maxes)
        w = jnp.exp(m_all - jnp.max(m_all, axis=0, keepdims=True))
        return jnp.sum(w * jnp.stack(nums), axis=0) / jnp.sum(w * jnp.stack(dens), axis=0)

    out = lax.map(one_block, (jnp.arange(nb), qb))
    return out.transpose(1, 2, 0, 3, 4).reshape(B, H, S, D).astype(v.dtype)

def hybrid_mixer(x, positions, w_in, b_forget, q_gain, kv_gain, w_uq, w_ukv, w_out):
    B, S, _ = x.shape
    h = x @ w_in
    cuts = np.cumsum(IN_SPLITS)[:-1].tolist()
    c_q, c_kv, k_rope, fox_qkv, fox_f, dil_qkv = jnp.split(h, cuts, axis=-1)

    q_a = to_heads(rms_norm(c_q, q_gain) @ w_uq, MLA_HEADS)
    kv_a = to_heads(rms_norm(c_kv, kv_gain) @ w_ukv, MLA_HEADS)
    q_a = jnp.concatenate([q_a[..., :MLA_NOPE_DIM], rope(q_a[..., MLA_NOPE_DIM:], positions)], axis=-1)
    k_r = jnp.broadcast_to(rope(k_rope[:, None], positions), (B, MLA_HEADS, S, MLA_ROPE_DIM))
    k_a = jnp.concatenate([kv_a[..., :MLA_NOPE_DIM], k_r], axis=-1)
    o_a = causal_block_attention(q_a, k_a, kv_a[..., MLA_NOPE_DIM:])

    q_b, k_b, v_b = [to_heads(t, FOX_HEADS) for t in jnp.split(fox_qkv, 3, axis=-1)]
    log_f = jax.nn.log_sigmoid(fox_f.astype(jnp.float32) + b_forget.astype(jnp.float32))
    cum_log_f = jnp.cumsum(log_f, axis=1).transpose(0, 2, 1)
    o_b = causal_block_attention(q_b, k_b, v_b, cum_log_f)

    q_c, k_c, v_c = [to_heads(t, DIL_HEADS) for t in jnp.split(dil_qkv, 3, axis=-1)]
    o_c = dilated_mixture_attention(rope(q_c, positions), rope(k_c, positions), v_c)

    mixed = jnp.concatenate([from_heads(o_a), from_heads(o_b), from_heads(o_c)], axis=-1)
    return mixed @ w_out

def memory_cross_attention(x, mem, w_q, w_kv, w_o):
    q = to_heads(x @ w_q, XATTN_HEADS).astype(jnp.float32)
    k, v = [to_heads(t, XATTN_HEADS).astype(jnp.float32) for t in jnp.split(mem @ w_kv, 2, axis=-1)]
    s = jnp.einsum('bhqd,bhkd->bhqk', q, k) * (q.shape[-1] ** -0.5)
    p = jax.nn.softmax(s, axis=-1)
    o = jnp.einsum('bhqk,bhkd->bhqd', p, v).astype(x.dtype)
    return from_heads(o) @ w_o

def shared_group_router(x, router_w, router_bias):
    B, S, _ = x.shape
    scores = jax.nn.sigmoid((x @ router_w).astype(jnp.float32))
    biased = scores + router_bias.astype(jnp.float32)
    grp = biased.reshape(B, S, N_GROUPS, EXPERTS_PER_GROUP)
    grp_score = jnp.sum(lax.top_k(grp, TOP_K)[0], axis=-1)
    g_sel = jnp.argmax(grp_score, axis=-1)
    in_group = g_sel[..., None] == jnp.arange(N_GROUPS)
    masked = jnp.where(in_group[..., None], grp, NEG_INF).reshape(B, S, N_EXPERTS)
    _, expert_idx = lax.top_k(masked, TOP_K)
    w = jnp.take_along_axis(scores, expert_idx, axis=-1)
    w = w / jnp.sum(w, axis=-1, keepdims=True)
    return jnp.sum(jax.nn.one_hot(expert_idx, N_EXPERTS, dtype=jnp.float32) * w[..., None], axis=-2)

def moe_ffn(x, gates, w_gate, w_up, w_down):
    def per_sequence(args):
        xs, gs = args
        hg = jnp.einsum('sd,edf->sef', xs, w_gate)
        hu = jnp.einsum('sd,edf->sef', xs, w_up)
        a = jax.nn.silu(hg) * hu * gs[..., None].astype(xs.dtype)
        return jnp.einsum('sef,efd->sd', a, w_down)
    return lax.map(per_sequence, (x, gates))

def setup_inputs(seed: int = 0) -> dict:
    key = jax.random.key(seed)
    ks = jax.random.split(key, 24)
    f32 = jnp.float32
    L = DEPTH

    def normal(k, shape, scale):
        return jax.random.normal(k, shape, f32) * scale

    def gain(k, shape):
        return 1.0 + 0.02 * jax.random.normal(k, shape, f32)

    def bias(k, shape):
        return 0.02 * jax.random.normal(k, shape, f32)

    beta = DEEPNORM_BETA
    positions = (jax.random.randint(ks[2], (BATCH, 1), 0, 1024, dtype=jnp.int32)
                 + jnp.arange(SEQ, dtype=jnp.int32)[None, :])
    return {
        "x": normal(ks[0], (BATCH, SEQ, D_MODEL), 1.0),
        "mem": normal(ks[1], (BATCH, N_MEM, D_MODEL), 1.0),
        "positions": positions,
        "w_in": normal(ks[3], (L, D_MODEL, IN_COLS), D_MODEL ** -0.5),
        "b_forget": FOX_GATE_BIAS_MEAN + 0.5 * jax.random.normal(ks[4], (L, FOX_HEADS), f32),
        "mla_q_gain": gain(ks[5], (L, MLA_Q_RANK)),
        "mla_kv_gain": gain(ks[6], (L, MLA_KV_RANK)),
        "mla_w_uq": normal(ks[7], (L, MLA_Q_RANK, MLA_HEADS * (MLA_NOPE_DIM + MLA_ROPE_DIM)), MLA_Q_RANK ** -0.5),
        "mla_w_ukv": normal(ks[8], (L, MLA_KV_RANK, MLA_HEADS * (MLA_NOPE_DIM + MLA_V_DIM)), MLA_KV_RANK ** -0.5),
        "w_mix_out": normal(ks[9], (L, D_MIX, D_MODEL), beta * D_MIX ** -0.5),
        "ln_mix_g": gain(ks[10], (L, D_MODEL)),
        "ln_mix_b": bias(ks[11], (L, D_MODEL)),
        "xattn_w_q": normal(ks[12], (L, D_MODEL, D_MODEL), D_MODEL ** -0.5),
        "xattn_w_kv": normal(ks[13], (L, D_MODEL, 2 * D_MODEL), D_MODEL ** -0.5),
        "xattn_w_o": normal(ks[14], (L, D_MODEL, D_MODEL), beta * D_MODEL ** -0.5),
        "ln_mem_g": gain(ks[15], (L, D_MODEL)),
        "ln_mem_b": bias(ks[16], (L, D_MODEL)),
        "router_w": normal(ks[17], (D_MODEL, N_EXPERTS), D_MODEL ** -0.5),
        "router_bias": normal(ks[18], (N_EXPERTS,), 0.01),
        "expert_w_gate": normal(ks[19], (L, N_EXPERTS, D_MODEL, D_EXPERT), D_MODEL ** -0.5),
        "expert_w_up": normal(ks[20], (L, N_EXPERTS, D_MODEL, D_EXPERT), D_MODEL ** -0.5),
        "expert_w_down": normal(ks[21], (L, N_EXPERTS, D_EXPERT, D_MODEL), beta * D_EXPERT ** -0.5),
        "ln_ffn_g": gain(ks[22], (L, D_MODEL)),
        "ln_ffn_b": bias(ks[23], (L, D_MODEL)),
    }

def reference(x, mem, positions, w_in, b_forget, mla_q_gain, mla_kv_gain, mla_w_uq, mla_w_ukv,
              w_mix_out, ln_mix_g, ln_mix_b, xattn_w_q, xattn_w_kv, xattn_w_o, ln_mem_g, ln_mem_b,
              router_w, router_bias, expert_w_gate, expert_w_up, expert_w_down, ln_ffn_g, ln_ffn_b):
    for l in range(DEPTH):
        mix = hybrid_mixer(x, positions, w_in[l], b_forget[l], mla_q_gain[l], mla_kv_gain[l],
                           mla_w_uq[l], mla_w_ukv[l], w_mix_out[l])
        x = layer_norm(DEEPNORM_ALPHA * x + mix, ln_mix_g[l], ln_mix_b[l])
        xa = memory_cross_attention(x, mem, xattn_w_q[l], xattn_w_kv[l], xattn_w_o[l])
        x = layer_norm(DEEPNORM_ALPHA * x + xa, ln_mem_g[l], ln_mem_b[l])
        gates = shared_group_router(x, router_w, router_bias)
        ff = moe_ffn(x, gates, expert_w_gate[l], expert_w_up[l], expert_w_down[l])
        x = layer_norm(DEEPNORM_ALPHA * x + ff, ln_ffn_g[l], ln_ffn_b[l])
    return x


_drawn_inputs = setup_inputs


def setup_inputs(seed=0):
    import zlib

    import numpy as np

    out = dict(_drawn_inputs(seed))
    spreads = {}
    factors = {'mla_q_gain': 8.0, 'mla_kv_gain': 3.905}
    for name, (base, spread) in spreads.items():
        noise = np.random.default_rng([zlib.crc32(name.encode()), seed]).standard_normal(out[name].shape)
        drawn = base * np.exp(spread * noise) if base else spread * noise
        out[name] = __import__('jax').numpy.asarray(drawn.astype(out[name].dtype))
    for name, factor in factors.items():
        out[name] = (out[name] * factor).astype(out[name].dtype)
    return out
```

```python
from contextlib import ExitStack

import numpy as np

import concourse.bass as bass
from concourse import mybir

F32 = mybir.dt.float32
F32R = mybir.dt.float32r
I32 = mybir.dt.int32
ALU = mybir.AluOpType
ACT = mybir.ActivationFunctionType
AX = mybir.AxisListType.X

P = 128
MLA_H, FOX_H, DIL_H, X_H = 4, 6, 6, 4
HD = 64
ROPE = 32
MLA_D, FOX_D, DIL_D = 96, 66, 64
QR, KVR = 256, 128
NE, NG, EPG, DE = 16, 4, 4, 256
DIL = ((128, 1), (512, 4), (2048, 16))
EPS = 1e-5
BIG = 1e30
THETA = 10000.0

RAW = 12
SPL = 4


class Signal:

    def __init__(self, sem, per, ahead=0):
        self.sem, self.per, self.ahead = sem, per, ahead

    def at(self, layer, count):
        return layer * self.per + (self.ahead + count)


def weight_stream():
    subs = []
    for name in ("A", "FQ"):
        subs += [(name, j, 0) for j in range(4)]
    subs += [("FK", j, 0) for j in range(4)]
    subs += [("UQ", 0, 0), ("UKV", 0, 0)]
    for name in ("FV", "DQ", "DK", "DV"):
        subs += [(name, j, 0) for j in range(4)]
    for name in ("MK0", "MK1", "MV0", "WO0", "WO1", "MV1", "XQ0", "XQ1", "XO0", "XO1"):
        subs += [(name, j, 0) for j in range(4)]
    subs += [("RT", j, 0) for j in range(2)]
    return subs


def build(nc, x, mem, positions, w_in, b_forget, mla_q_gain, mla_kv_gain, mla_w_uq, mla_w_ukv, w_mix_out,
          ln_mix_g, ln_mix_b, xattn_w_q, xattn_w_kv, xattn_w_o, ln_mem_g, ln_mem_b, router_w, router_bias,
          expert_w_gate, expert_w_up, expert_w_down, ln_ffn_g, ln_ffn_b, out):
    _, T, DM = x.shape
    L = w_in.shape[0]
    TT = T // P
    KC = DM // P
    assert TT == 2 and KC == 8 and mem.shape[1] == T
    ALPHA = float((2 * L) ** 0.25)
    HEADS = MLA_H + FOX_H + DIL_H

    c = 0
    cols = {}
    for name, width in (("CQ", QR), ("CKV", KVR), ("KR", ROPE), ("FQ", FOX_H * HD), ("FK", FOX_H * HD),
                        ("FV", FOX_H * HD), ("FF", FOX_H), ("DQ", DIL_H * HD), ("DK", DIL_H * HD),
                        ("DV", DIL_H * HD)):
        cols[name] = (c, width)
        c += width
    A_W = QR + KVR + ROPE
    A_ALL = A_W + FOX_H

    stream = weight_stream()
    index = {}
    for i, (name, j, _) in enumerate(stream):
        index[name, j] = i
    N1 = len(stream)
    N_PRO, N_BODY, N_EPI = 8, 12, 4
    TURNS = NE // 2 - 1
    NSUB = N1 + N_PRO + TURNS * N_BODY + N_EPI
    assert N1 % RAW == 0 and NSUB % RAW == 0 and N_BODY % RAW == 0

    def width(i):
        name = stream[i][0]
        if name == "A":
            return 2 * A_ALL
        if name in cols:
            return 2 * cols[name][1]
        return {"UQ": 768, "UKV": 512, "RT": 64}.get(name, 1024)

    def brings(i):
        return 32 if i < N1 and stream[i][0] == "A" else 16

    body_brings = [32] * 4 + [16] * 4 + [32] * 4
    landed_value, slot_total = [], [0] * RAW
    for i in range(N1):
        slot_total[i % RAW] += brings(i)
        landed_value.append(slot_total[i % RAW])
    for j in range(N_PRO):
        slot_total[(N1 + j) % RAW] += 32
        landed_value.append(slot_total[(N1 + j) % RAW])
    body_start = [slot_total[(N_PRO + j) % RAW] + body_brings[j] for j in range(N_BODY)]
    for j in range(N_BODY):
        slot_total[(N_PRO + j) % RAW] += TURNS * body_brings[j]
    epi_value = []
    for j in range(N_EPI):
        slot = (N_PRO + TURNS * N_BODY + j) % RAW
        slot_total[slot] += 16
        epi_value.append(slot_total[slot])

    with ExitStack() as ctx:
        base = -(-nc.sbuf_base // 64) * 64
        place = [base]

        def sb(name, shape, dt=F32, at=None):
            size = int(np.prod(shape[1:])) * 4
            size = -(-size // 64) * 64
            if at is None:
                at = place[0]
                place[0] += size
            return nc.alloc_sbuf_tensor_at(name, shape, dt, offset=at), at + size

        raw, _ = sb("raw", [P, RAW, 1024])
        w_hi, _ = sb("w_hi", [P, SPL, 1024], F32R)
        w_lo, _ = sb("w_lo", [P, SPL, 1024], F32R)
        xs, _ = sb("xs", [P, TT, DM])
        xT_hi, _ = sb("xT_hi", [P, KC, T], F32R)
        xT_lo, _ = sb("xT_lo", [P, KC, T], F32R)
        memT_hi, _ = sb("memT_hi", [P, KC, T], F32R)
        memT_lo, _ = sb("memT_lo", [P, KC, T], F32R)
        gb, _ = sb("gb", [P, 2, DM])
        ident, _ = sb("ident", [P, P])
        causal, _ = sb("causal", [P, 2 * P])
        dilmask, _ = sb("dilmask", [P, 2 * P])
        dilcount, _ = sb("dilcount", [P, 2 * P])
        upto, _ = sb("upto", [P, P])
        ones, _ = sb("ones", [P, P])
        cosb, _ = sb("cosb", [P, TT, 32])
        sinb, _ = sb("sinb", [P, TT, 32])
        gains, _ = sb("gains", [P, QR + KVR])
        bforget, _ = sb("bforget", [P, FOX_H])
        rbias, _ = sb("rbias", [P, NE])
        mhalf, _ = sb("mhalf", [P, 4])
        nmean, _ = sb("nmean", [P, 1])
        st, _ = sb("st", [P, 8, 4])
        mx, _ = sb("mx", [P, HEADS + X_H, TT])
        nmx, _ = sb("nmx", [P, HEADS + X_H, TT])
        sm, _ = sb("sm", [P, HEADS + X_H, TT])
        sm1, _ = sb("sm1", [P, HEADS, TT])
        ri, _ = sb("ri", [P, HEADS + X_H, TT])
        gates, _ = sb("gates", [P, TT, NE])
        desc16, _ = sb("desc16", [P, TT * NE])
        desc4, _ = sb("desc4", [P, TT * NG])
        work = place[0]

        mixT_hi, _ = sb("mixT_hi", [P, KC, T], F32R)
        mixT_lo, _ = sb("mixT_lo", [P, KC, T], F32R)
        mq, _ = sb("mq", [P, TT, MLA_H, MLA_D])
        q_work = place[0]
        mk, _ = sb("mk", [P, TT, MLA_H, MLA_D])
        mv, _ = sb("mv", [P, TT, MLA_H, HD])
        fq, _ = sb("fq", [P, TT, FOX_H, FOX_D])
        fk, _ = sb("fk", [P, TT, FOX_H, FOX_D])
        fv, _ = sb("fv", [P, TT, FOX_H, HD])
        dq, _ = sb("dq", [P, TT, DIL_H, HD])
        dk, _ = sb("dk", [P, TT, DIL_H, HD])
        dv, _ = sb("dv", [P, TT, DIL_H, HD])
        kv_work = place[0]
        kTx, _ = sb("kTx", [P, KC, T])
        vx, _ = sb("vx", [P, TT, DM])
        head_work = place[0]
        qkT, _ = sb("qkT", [P, 2, 4 * P])
        p_sb, _ = sb("p_sb", [P, 2, 4 * P])
        pT, _ = sb("pT", [P, 2, 4 * P])
        used = place[0]
        junk, _ = sb("junk", [P, DM], at=head_work)
        lat, _ = sb("lat", [P, TT, QR + KVR], at=head_work)
        latT_hi, e2 = sb("latT_hi", [P, 3, T], F32R, at=kv_work)
        latT_lo, e3 = sb("latT_lo", [P, 3, T], F32R, at=e2)
        rot, e5 = sb("rot", [P, 2, 2, TT * DIL_H * 32], at=kv_work + 8192)
        assert e3 <= kv_work + 8192 and e5 <= head_work
        kf, _ = sb("kf", [P, TT, ROPE + FOX_H])
        fz, _ = sb("fz", [P, 4, TT * FOX_H])
        qTx, e4 = sb("qTx", [P, KC, T], at=q_work)
        act_a, m1 = sb("act_a", [P, 2, TT, DE], at=work)
        silu, m2 = sb("silu", [P, 2, TT, DE], at=m1)
        aT_hi, m3 = sb("aT_hi", [P, 2, 2, T], F32R, at=m2)
        aT_lo, m4 = sb("aT_lo", [P, 2, 2, T], F32R, at=m3)
        zero1, m5 = sb("zero1", [P, 512], mybir.dt.bfloat16, at=m4)
        rt, m6 = sb("rt", [P, 24, TT * NE], at=m5)
        logitT, m7 = sb("logitT", [P, T], at=m6)
        assert m7 <= used
        mem_tok, _ = sb("mem_tok", [P, TT, DM], at=work)
        pos_i, b1 = sb("pos_i", [P, TT], I32, at=work + 8192)
        ang, b2 = sb("ang", [P, 8, TT * 32], at=b1)
        freq, b3 = sb("freq", [P, TT, 32], at=b2)
        offs, b4 = sb("offs", [P, 2 * P], I32, at=b3)
        offs2, b5 = sb("offs2", [P, 2 * P], I32, at=b4)
        offf, b6 = sb("offf", [P, 3, 2 * P], at=b5)
        assert b6 <= used and place[0] <= nc.sbuf_usable_end, (place[0], nc.sbuf_usable_end)

        bank = [ctx.enter_context(nc.psum_tensor(f"bank{i}", [P, 512], F32)) for i in range(8)]
        B_QK, B_S, B_PT, B_O = bank[4], bank[5], bank[6], bank[7]

        def sem(name):
            return ctx.enter_context(nc.semaphore(name))

        def signal(name, per, ahead=0):
            return Signal(sem(name), per, ahead)

        jobs = [("XT0", 2, 2), ("XT1", 2, 2), ("A", 6, 4), ("FQ", 2, 0), ("FK", 0, 2), ("LT", 2, 6),
                ("UQ", 2, 0), ("UKV", 0, 4), ("FV", 2, 0), ("DQ", 2, 0), ("DK", 2, 0), ("DV", 0, 2),
                ("MK0", 2, 0), ("MK1", 2, 0), ("MV0", 0, 2), ("WO0", 0, 2), ("WO1", 0, 2), ("MV1", 0, 2),
                ("XT0b", 2, 2), ("XT1b", 2, 2), ("XQ0", 2, 0), ("XQ1", 2, 0), ("XO0", 0, 2), ("XO1", 0, 2),
                ("XT0c", 2, 2), ("XT1c", 2, 2), ("RT", 1, 0), ("GT", 1, 0)]
        job = {name: n for n, (name, _, _) in enumerate(jobs)}
        pair = {}
        for n, (name, _, _) in enumerate(jobs):
            pair[name] = n % 2
        evac_a = np.cumsum([a for _, a, _ in jobs]).tolist()
        evac_v = np.cumsum([v for _, _, v in jobs]).tolist()

        turning = ["XT0", "XT1", "LT", "XT0b", "XT1b", "XT0c", "XT1c", "GT"]
        last_sub = {name: index[name, j] for name, j in index}

        def job_done(l, name):
            if name in turning:
                return turned.sem, turned.at(l, turning.index(name) + 1)
            return split_free.sem, split_free.at(l, last_sub[name] + 1)

        def banks(name):
            return [bank[2 * pair[name]], bank[2 * pair[name] + 1]]

        raw_in = [Signal(sem(f"raw_in{i}"), slot_total[i]) for i in range(RAW)]
        hi_ready = signal("hi_ready", NSUB)
        lo_ready = signal("lo_ready", NSUB, RAW)
        split_free = signal("split_free", NSUB, SPL)
        turned = signal("turned", 8)
        job_a = signal("job_a", evac_a[-1])
        job_v = signal("job_v", evac_v[-1])
        x_ready = signal("x_ready", 6, 2)
        ln_sum = signal("ln_sum", 6)
        ln_nmean = signal("ln_nmean", 6)
        ln_sq = signal("ln_sq", 6)
        ln_rstd = signal("ln_rstd", 12)
        ln_scaled = signal("ln_scaled", 6)
        gb_in = signal("gb_in", 96)
        small_in = signal("small_in", 48)
        qk_done = signal("qk_done", HEADS)
        qkT_ready = signal("qkT_ready", HEADS)
        s_done = signal("s_done", HEADS + X_H)
        s_masked = signal("s_masked", 2 * HEADS + X_H)
        nmx_ready = signal("nmx_ready", HEADS + X_H)
        e_ready = signal("e_ready", 2 * (HEADS + X_H))
        counted = signal("counted", 2 * DIL_H)
        ri_ready = signal("ri_ready", HEADS + X_H)
        p_ready = signal("p_ready", 2 * (HEADS + X_H))
        pt_done = signal("pt_done", HEADS + X_H)
        pT_ready = signal("pT_ready", HEADS + X_H)
        acc_read = signal("acc_read", 4)
        o_done = signal("o_done", HEADS + X_H)
        o_hi = signal("o_hi", HEADS // 2 + X_H)
        o_lo = signal("o_lo", HEADS // 2 + X_H)
        rms_step = signal("rms_step", 2)
        fz_v = signal("fz_v", 3)
        fz_a = signal("fz_a", 2)
        aug = signal("aug", 2)
        rope_step = signal("rope_step", 26)
        route = signal("route", 39)
        acc_zero = signal("acc_zero", 1)
        silu_ready = signal("silu_ready", 2 * NE)
        a_ready = signal("a_ready", 2 * NE)
        at_done = signal("at_done", NE)
        aT_a = signal("aT_a", NE)
        aT_v = signal("aT_v", NE)
        start_in = sem("start_in")
        paused_v, paused_p, paused_t = sem("paused_v"), sem("paused_p"), sem("paused_t")
        pos_in = sem("pos_in")
        const_pool = sem("const_pool")
        const_v = sem("const_v")
        const_a = sem("const_a")
        angles = sem("angles")
        tables = sem("tables")
        mem_done = sem("mem_done")
        mem_a = sem("mem_a")
        mem_v = sem("mem_v")
        out_sent = sem("out_sent")

        feat = lambda w: w.rearrange("(k p) n -> p k n", p=P)

        slots = [1] * 8 + [2] * 2 + [2, 2, 2] + [1] * 6
        fill = [index["DQ", 0] + i for i in range(24)]
        assert sum(slots) == len(fill)
        turns, k = [], 0
        for n in slots:
            turns.append(fill[k:k + n])
            k += n
        assert len(turns) == HEADS + 3
        xturns = [[index["XQ1", 0], index["XQ1", 1]], [index["XQ1", 2], index["XQ1", 3]], [], [], [], [], []][:X_H + 2]

        def lookahead():
            nxt = []
            for n in range(len(turns)):
                nxt.append(turns[n + 1] if n + 1 < len(turns) else [index["WO0", 0], index["WO0", 1]])
            return nxt
        ahead_of = lookahead()

        block = ctx.enter_context(nc.Block())

        @block.sync
        def _(sp):
            sp.dma_start(xs[:, :, :], x[0].rearrange("(t p) d -> p t d", p=P)).then_inc(start_in, 16)
            sp.dma_start(mem_tok[:, :, :], mem[0].rearrange("(t p) d -> p t d", p=P)).then_inc(start_in, 16)

            def load(l, i, slot, pieces, value=None):
                sp.wait_ge(lo_ready.sem, lo_ready.at(l, i - RAW + 1))
                for dst, src in pieces:
                    sp.dma_start(dst, src).then_inc(raw_in[slot].sem, 16)

            def straight(l, i):
                name, j, _ = stream[i]
                slot = i % RAW
                row = raw[:, slot, 0:width(i)]
                if name == "A":
                    r = row.rearrange("p (k n) -> p k n", k=2)
                    w = feat(w_in[l])[:, 2 * j:2 * j + 2, :]
                    f0 = cols["FF"][0]
                    return [(r[:, :, 0:A_W], w[:, :, 0:A_W]), (r[:, :, A_W:A_ALL], w[:, :, f0:f0 + FOX_H])]
                if name in cols:
                    c0, n = cols[name]
                    return [(row.rearrange("p (k n) -> p k n", k=2), feat(w_in[l])[:, 2 * j:2 * j + 2, c0:c0 + n])]
                if name == "UQ":
                    return [(row.rearrange("p (k n) -> p k n", k=2), feat(mla_w_uq[l]))]
                if name == "UKV":
                    return [(row, mla_w_ukv[l])]
                if name == "RT":
                    return [(row.rearrange("p (k n) -> p k n", k=4), feat(router_w)[:, 4 * j:4 * j + 4, :])]
                src, c0 = {"MK0": (xattn_w_kv, 0), "MK1": (xattn_w_kv, 512), "MV0": (xattn_w_kv, 1024),
                           "MV1": (xattn_w_kv, 1536), "WO0": (w_mix_out, 0), "WO1": (w_mix_out, 512),
                           "XQ0": (xattn_w_q, 0), "XQ1": (xattn_w_q, 512), "XO0": (xattn_w_o, 0),
                           "XO1": (xattn_w_o, 512)}[name]
                return [(row.rearrange("p (k n) -> p k n", k=2), feat(src[l])[:, 2 * j:2 * j + 2, c0:c0 + 512])]

            def up(l, e, i, slot0):
                for j in range(4):
                    slot = (slot0 + j) % RAW
                    r = raw[:, slot, :].rearrange("p (k g n) -> p k g n", k=2, g=2)
                    load(l, i + j, slot, [(r[:, :, g, :], feat(w[l][e])[:, 2 * j:2 * j + 2, :])
                                          for g, w in enumerate((expert_w_gate, expert_w_up))])

            def down(l, e, i, slot0):
                for j in range(2):
                    slot = (slot0 + j) % RAW
                    load(l, i + j, slot, [(raw[:, slot, :], expert_w_down[l][e][j * P:(j + 1) * P, :])])

            with sp.Fori(0, L) as l:
                for i in range(N1):
                    load(l, i, i % RAW, straight(l, i))
                up(l, 0, N1, 0)
                up(l, 1, N1 + 4, 4)
                with sp.Fori(0, TURNS) as p:
                    i = p * N_BODY + (N1 + N_PRO)
                    up(l, p * 2 + 2, i, N_PRO)
                    down(l, p * 2, i + 4, N_PRO + 4)
                    down(l, p * 2 + 1, i + 6, N_PRO + 6)
                    up(l, p * 2 + 3, i + 8, N_PRO + 8)
                down(l, NE - 2, NSUB - 4, N_PRO)
                down(l, NE - 1, NSUB - 2, N_PRO + 2)
            sp.wait_ge(x_ready.sem, x_ready.at(L - 1, 6))
            sp.dma_start(out[0].rearrange("(t p) d -> p t d", p=P), xs[:, :, :]).then_inc(out_sent, 16)
            sp.wait_ge(out_sent, 16)

        def where(l, i, p=None):
            if p is not None:
                slot = (N_PRO + i) % RAW
                return slot, raw_in[slot].sem, p * body_brings[i] + raw_in[slot].at(l, body_start[i])
            if i >= NSUB - N_EPI:
                j = i - (NSUB - N_EPI)
                slot = (N_PRO + j) % RAW
                return slot, raw_in[slot].sem, raw_in[slot].at(l, epi_value[j])
            return i % RAW, raw_in[i % RAW].sem, raw_in[i % RAW].at(l, landed_value[i])

        def number(i, p):
            return i if p is None else p * N_BODY + (N1 + N_PRO + i)

        def split_hi(act, l, i, p=None):
            slot, landed, value = where(l, i, p)
            n, w = number(i, p), (width(i) if p is None and i < N1 else 1024)
            act.wait_ge(landed, value)
            act.wait_ge(split_free.sem, split_free.at(l, n - SPL + 1))
            nc.scalar.activation(w_hi[:, i % SPL, 0:w], raw[:, slot, 0:w], ACT.Copy).then_inc(hi_ready.sem, 1)

        def split_lo(dve, l, i, p=None):
            slot, landed, value = where(l, i, p)
            n, w = number(i, p), (width(i) if p is None and i < N1 else 1024)
            dve.wait_ge(hi_ready.sem, hi_ready.at(l, n + 1))
            nc.vector.tensor_tensor(w_lo[:, i % SPL, 0:w], raw[:, slot, 0:w],
                                    w_hi[:, i % SPL, 0:w].bitcast(F32), ALU.subtract).then_inc(lo_ready.sem, 1)

        @block.gpsimd
        def _(pool):
            pool.dma_start(pos_i[:, :], positions[0].rearrange("(t p) -> p t", p=P),
                           allow_slow_non_contiguous=True).then_inc(pos_in, 16)
            pool.dma_start(rbias[:, :], router_bias.rearrange("(a n) -> a n", a=1).to_broadcast([P, NE])).then_inc(pos_in, 16)
            nc.gpsimd.memset(ident[:, :], 0.0).then_inc(const_pool, 1)
            nc.gpsimd.memset(causal[:, :], 0.0).then_inc(const_pool, 1)
            nc.gpsimd.memset(upto[:, :], 1.0).then_inc(const_pool, 1)
            nc.gpsimd.memset(ones[:, :], 1.0).then_inc(const_pool, 1)
            nc.gpsimd.memset(mhalf[:, :], -0.5).then_inc(const_pool, 1)
            nc.gpsimd.memset(nmean[:, :], -1.0 / DM).then_inc(const_pool, 1)
            inv = (np.float32(THETA) ** (-np.arange(32, dtype=np.float32) / np.float32(32))).astype(np.float32)
            for i in range(32):
                nc.gpsimd.memset(freq[:, :, i:i + 1], float(inv[i])).then_inc(const_pool, 1)
            pool.wait_ge(const_pool, 38)
            nc.gpsimd.affine_select(out=ident[:, :], in_=ident[:, :], compare_op=ALU.not_equal, fill=1.0, base=0,
                                    pattern=[[-1, P]], channel_multiplier=1).then_inc(const_pool, 1)
            nc.gpsimd.affine_select(out=upto[:, :], in_=upto[:, :], compare_op=ALU.is_ge, fill=0.0, base=0,
                                    pattern=[[1, P]], channel_multiplier=-1).then_inc(const_pool, 1)
            nc.gpsimd.affine_select(out=causal[:, :], in_=causal[:, :], compare_op=ALU.is_ge, fill=-BIG,
                                    base=P, pattern=[[-1, 2 * P]], channel_multiplier=1).then_inc(const_pool, 1)
            nc.gpsimd.iota(offs[:, :], pattern=[[-1, 2 * P]], base=1024 + P, channel_multiplier=1)\
                .then_inc(const_pool, 1)
            nc.gpsimd.iota(desc16[:, :], pattern=[[0, TT], [-1, NE]], base=NE, channel_multiplier=0,
                           allow_small_or_imprecise_dtypes=True).then_inc(const_pool, 1)
            nc.gpsimd.iota(desc4[:, :], pattern=[[0, TT], [-1, NG]], base=NG, channel_multiplier=0,
                           allow_small_or_imprecise_dtypes=True).then_inc(const_pool, 1)

            def rotate(l, dst, src, n_heads, half, step, n0):
                shape = [P, TT, n_heads, half]
                c_ = cosb[:, :, 0:32:step].unsqueeze(2).to_broadcast(shape)
                s_ = sinb[:, :, 0:32:step].unsqueeze(2).to_broadcast(shape)
                x1, x2 = src[:, :, :, 0:half], src[:, :, :, half:2 * half]
                n = TT * n_heads * half
                t = [rot[:, i, j, 0:n].rearrange("p (t h d) -> p t h d", t=TT, h=n_heads) for i in range(2) for j in range(2)]
                if n0:
                    pool.wait_ge(rope_step.sem, rope_step.at(l, n0))
                nc.gpsimd.tensor_tensor(t[0], x1, c_, ALU.mult).then_inc(rope_step.sem, 1)
                nc.gpsimd.tensor_tensor(t[1], x2, s_, ALU.mult).then_inc(rope_step.sem, 1)
                nc.gpsimd.tensor_tensor(t[2], x1, s_, ALU.mult).then_inc(rope_step.sem, 1)
                nc.gpsimd.tensor_tensor(t[3], x2, c_, ALU.mult).then_inc(rope_step.sem, 1)
                pool.wait_ge(rope_step.sem, rope_step.at(l, n0 + 4))
                nc.gpsimd.tensor_tensor(dst[:, :, :, 0:half], t[0], t[1], ALU.subtract).then_inc(rope_step.sem, 1)
                nc.gpsimd.tensor_tensor(dst[:, :, :, half:2 * half], t[2], t[3], ALU.add).then_inc(rope_step.sem, 1)

            def norm(l, n, g_dram, b_dram):
                pool.wait_ge(x_ready.sem, x_ready.at(l, 2 * n))
                pool.nop().then_inc(paused_p, 1)
                for r, d in enumerate((g_dram, b_dram)):
                    pool.dma_start(gb[:, r, :], d[l].rearrange("(a n) -> a n", a=1).to_broadcast([P, DM]))\
                        .then_inc(gb_in.sem, 16)

            def deviation(l, n):
                for t in range(TT):
                    k = 2 * n + t
                    pool.wait_ge(ln_sq.sem, ln_sq.at(l, k + 1))
                    pool.nop().then_inc(paused_p, 1)
                    nc.gpsimd.tensor_scalar(st[:, k, 2:3], st[:, k, 2:3], 1.0 / DM, EPS, ALU.mult, ALU.add)\
                        .then_inc(ln_rstd.sem, 1)
                    pool.wait_ge(ln_rstd.sem, ln_rstd.at(l, 2 * k + 1))
                    nc.gpsimd.tensor_tensor(st[:, k, 3:4], st[:, k, 2:3], mhalf[:, 0:1], ALU.pow)\
                        .then_inc(ln_rstd.sem, 1)

            pool.wait_ge(tables, 1)
            with pool.Fori(0, L) as l:
                norm(l, 0, ln_mix_g, ln_mix_b)
                pool.dma_start(gains[:, 0:QR], mla_q_gain[l].rearrange("(a n) -> a n", a=1).to_broadcast([P, QR]))\
                    .then_inc(small_in.sem, 16)
                pool.dma_start(gains[:, QR:QR + KVR],
                               mla_kv_gain[l].rearrange("(a n) -> a n", a=1).to_broadcast([P, KVR]))\
                    .then_inc(small_in.sem, 16)
                pool.dma_start(bforget[:, :], b_forget[l].rearrange("(a n) -> a n", a=1).to_broadcast([P, FOX_H]))\
                    .then_inc(small_in.sem, 16)
                nc.gpsimd.memset(fq[:, :, :, HD + 1:HD + 2], 1.0).then_inc(aug.sem, 1)
                nc.gpsimd.memset(fk[:, :, :, HD:HD + 1], 1.0).then_inc(aug.sem, 1)
                pool.wait_ge(job_a.sem, job_a.at(l, evac_a[job["A"]]))
                pool.nop().then_inc(paused_p, 1)
                sq = sm1[:, 0:2, :]
                nc.gpsimd.tensor_scalar(sq, sq, 1.0, EPS, ALU.mult, ALU.add).then_inc(rms_step.sem, 1)
                pool.wait_ge(rms_step.sem, rms_step.at(l, 1))
                nc.gpsimd.tensor_tensor(sm1[:, 2:4, :], sq, mhalf[:, :].rearrange("p (a b) -> p a b", a=2), ALU.pow)\
                    .then_inc(rms_step.sem, 1)
                kr = kf[:, :, 0:ROPE].unsqueeze(2)
                rotate(l, kr, kr, 1, 16, 2, 0)
                pool.wait_ge(job_a.sem, job_a.at(l, evac_a[job["UQ"]]))
                rotate(l, mq[:, :, :, HD:HD + ROPE], mq[:, :, :, HD:HD + ROPE], MLA_H, 16, 2, 6)
                for t in range(TT):
                    nc.gpsimd.tensor_copy(mk[:, t, :, HD:HD + ROPE],
                                          kf[:, t, 0:ROPE].unsqueeze(1).to_broadcast([P, MLA_H, ROPE]))\
                        .then_inc(rope_step.sem, 1)
                for n, (name, q) in enumerate((("DQ", dq), ("DK", dk))):
                    pool.wait_ge(job_a.sem, job_a.at(l, evac_a[job[name]]))
                    rotate(l, q[:, :, :, :], q[:, :, :, :], DIL_H, 32, 1, 14 + 6 * n)
                deviation(l, 0)
                norm(l, 1, ln_mem_g, ln_mem_b)
                deviation(l, 1)
                nc.gpsimd.memset(zero1[:, :], 0.0).then_inc(acc_zero.sem, 1)
                norm(l, 2, ln_ffn_g, ln_ffn_b)
                deviation(l, 2)

        @block.scalar
        def _(act):
            act.wait_ge(angles, 1)
            nc.scalar.activation(sinb[:, :, :].rearrange("p t d -> p (t d)"), ang[:, 6, :], ACT.Sin).then_inc(const_a, 1)
            nc.scalar.activation(cosb[:, :, :].rearrange("p t d -> p (t d)"), ang[:, 7, :], ACT.Sin).then_inc(const_a, 1)
            for n in range(4):
                act.wait_ge(mem_done, n + 1)
                t, h = n // 2, n % 2
                nc.scalar.activation(memT_hi[:, 4 * h:4 * h + 4, t * P:(t + 1) * P],
                                     bank[n][:, :].rearrange("p (k m) -> p k m", k=4), ACT.Copy).then_inc(mem_a, 1)

            def wait_job(l, name):
                act.wait_ge(*job_done(l, name))

            def turn_x(l, name, t):
                wait_job(l, name)
                for h, b in enumerate(banks(name)):
                    nc.scalar.activation(xT_hi[:, 4 * h:4 * h + 4, t * P:(t + 1) * P],
                                         b[:, :].rearrange("p (k m) -> p k m", k=4), ACT.Copy).then_inc(job_a.sem, 1)

            def copy_job(l, name, dst, w):
                wait_job(l, name)
                for t, b in enumerate(banks(name)):
                    nc.scalar.activation(dst(t), w(b), ACT.Copy).then_inc(job_a.sem, 1)

            def heads_of(b, n, d):
                return b[:, 0:n * d].rearrange("p (h d) -> p h d", h=n)

            def evac_qk(l, h):
                act.wait_ge(qk_done.sem, qk_done.at(l, h + 1))
                if h >= 2:
                    act.wait_ge(s_done.sem, s_done.at(l, h - 1))
                d = MLA_D if h < MLA_H else FOX_D if h < MLA_H + FOX_H else DIL_D
                nc.scalar.activation(qkT[0:d, h % 2, :], B_QK[0:d, :], ACT.Copy).then_inc(qkT_ready.sem, 1)

            def exps(l, h):
                act.wait_ge(nmx_ready.sem, nmx_ready.at(l, h + 1))
                if h >= 2:
                    act.wait_ge(pt_done.sem, pt_done.at(l, h - 1))
                for t in range(TT):
                    if h < HEADS:
                        sl = slice(0, P) if t == 0 else slice(P, 3 * P)
                        src, scale = p_sb[:, h % 2, sl], 1.0
                    else:
                        sl = slice(t * T, (t + 1) * T)
                        src, scale = B_S[:, sl], 1.0 / 16.0
                    acc = sm1 if MLA_H + FOX_H <= h < HEADS else sm
                    nc.scalar.activation(p_sb[:, h % 2, sl], src, ACT.Exp, bias=nmx[:, h, t:t + 1], scale=scale,
                                         accum_out=acc[:, h, t:t + 1]).then_inc(e_ready.sem, 1)

            def evac_o(l, h):
                if h < HEADS:
                    n = h // 2
                    act.wait_ge(o_done.sem, o_done.at(l, h + 1))
                    nc.scalar.activation(mixT_hi[:, n, :], B_O[:, 0:T], ACT.Copy).then_inc(o_hi.sem, 1)
                else:
                    n = h - HEADS
                    act.wait_ge(o_done.sem, o_done.at(l, h + 1))
                    nc.scalar.activation(mixT_hi[:, 2 * n:2 * n + 2, :],
                                         B_O[:, :].rearrange("p (c t) -> p c t", c=2), ACT.Copy).then_inc(o_hi.sem, 1)

            def square(l, n):
                for t in range(TT):
                    k = 2 * n + t
                    act.wait_ge(ln_nmean.sem, ln_nmean.at(l, k + 1))
                    if k:
                        act.wait_ge(ln_sq.sem, ln_sq.at(l, k))
                    nc.scalar.activation(junk[:, :], xs[:, t, :], ACT.Square, bias=st[:, k, 1:2],
                                         accum_out=st[:, k, 2:3]).then_inc(ln_sq.sem, 1)

            def silu_of(l, par, used):
                act.wait_ge(split_free.sem, split_free.at(l, used))
                for t in range(TT):
                    nc.scalar.activation(silu[:, par, t, :], bank[4 + 2 * par + t][:, 0:DE], ACT.Silu)\
                        .then_inc(silu_ready.sem, 1)

            def aT_of(l, e, par):
                act.wait_ge(at_done.sem, at_done.at(l, e + 1))
                nc.scalar.activation(aT_hi[:, par, :, :], bank[6 + par][:, :].rearrange("p (c t) -> p c t", c=2),
                                     ACT.Copy).then_inc(aT_a.sem, 1)

            act.wait_ge(tables, 1)
            with act.Fori(0, L) as l:
                for i in range(0, 4):
                    split_hi(act, l, i)
                turn_x(l, "XT0", 0)
                turn_x(l, "XT1", 1)
                for i in range(4, 8):
                    split_hi(act, l, i)
                wait_job(l, "A")
                for t, b in enumerate(banks("A")):
                    for g, (c0, n) in enumerate(((0, QR), (QR, KVR))):
                        nc.scalar.activation(junk[:, t * 512 + c0:t * 512 + c0 + n], b[:, c0:c0 + n], ACT.Square,
                                             scale=float(n) ** -0.5, accum_out=sm1[:, g, t:t + 1]).then_inc(job_a.sem, 1)
                    nc.scalar.activation(kf[:, t, :], b[:, QR + KVR:A_ALL], ACT.Copy).then_inc(job_a.sem, 1)
                for i in range(8, 10):
                    split_hi(act, l, i)
                act.wait_ge(fz_v.sem, fz_v.at(l, 2))
                nc.scalar.activation(fz[:, 2, :], fz[:, 1, :], ACT.Exp, scale=-1.0).then_inc(fz_a.sem, 1)
                act.wait_ge(fz_a.sem, fz_a.at(l, 1))
                nc.scalar.activation(fz[:, 3, :], fz[:, 2, :], ACT.Ln, bias=1.0).then_inc(fz_a.sem, 1)
                for i in range(10, 12):
                    split_hi(act, l, i)
                copy_job(l, "FQ", lambda t: fq[:, t, :, 0:HD], lambda b: heads_of(b, FOX_H, HD))
                wait_job(l, "LT")
                for t, b in enumerate(banks("LT")):
                    nc.scalar.activation(latT_hi[:, :, t * P:(t + 1) * P],
                                         b[:, 0:3 * P].rearrange("p (k m) -> p k m", k=3), ACT.Copy).then_inc(job_a.sem, 1)
                for i in range(12, 18):
                    split_hi(act, l, i)
                    if i == 14:
                        copy_job(l, "UQ", lambda t: mq[:, t, :, :], lambda b: heads_of(b, MLA_H, MLA_D))
                split_hi(act, l, 18)
                copy_job(l, "FV", lambda t: fv[:, t, :, :], lambda b: heads_of(b, FOX_H, HD))
                done = 19
                for s in range(HEADS + 3):
                    target = ahead_of[s]
                    for i in target:
                        if i >= done:
                            split_hi(act, l, i)
                            done = i + 1
                    if index["DQ", 3] in turns[s]:
                        copy_job(l, "DQ", lambda t: dq[:, t, :, :], lambda b: heads_of(b, DIL_H, HD))
                    if index["DK", 3] in turns[s]:
                        copy_job(l, "DK", lambda t: dk[:, t, :, :], lambda b: heads_of(b, DIL_H, HD))
                    for nm, r in (("MK0", 0), ("MK1", 1)):
                        if index[nm, 3] in turns[s]:
                            wait_job(l, nm)
                            for u, b in enumerate(banks(nm)):
                                nc.scalar.activation(kTx[:, 4 * r + 2 * u:4 * r + 2 * u + 2, :],
                                                     b[:, :].rearrange("p (c t) -> p c t", c=2), ACT.Copy)\
                                    .then_inc(job_a.sem, 1)
                    if s < HEADS:
                        evac_qk(l, s)
                    if 1 <= s <= HEADS:
                        exps(l, s - 1)
                    if s >= 3 and (s - 3) % 2 == 1:
                        evac_o(l, s - 3)
                for i in range(done, index["XQ0", 0]):
                    split_hi(act, l, i)
                square(l, 0)
                for i in range(index["XQ0", 0], index["XQ1", 0]):
                    split_hi(act, l, i)
                turn_x(l, "XT0b", 0)
                turn_x(l, "XT1b", 1)
                for i in range(index["XQ1", 0], index["XQ1", 3] + 1):
                    split_hi(act, l, i)
                    if i == index["XQ1", 1]:
                        wait_job(l, "XQ0")
                        for u, b in enumerate(banks("XQ0")):
                            nc.scalar.activation(qTx[:, 2 * u:2 * u + 2, :], b[:, :].rearrange("p (c t) -> p c t", c=2),
                                                 ACT.Copy).then_inc(job_a.sem, 1)
                for s in range(X_H + 2):
                    if s == 1:
                        wait_job(l, "XQ1")
                        for u, b in enumerate(banks("XQ1")):
                            nc.scalar.activation(qTx[:, 4 + 2 * u:6 + 2 * u, :],
                                                 b[:, :].rearrange("p (c t) -> p c t", c=2), ACT.Copy)\
                                .then_inc(job_a.sem, 1)
                    if s < X_H:
                        exps(l, HEADS + s)
                    if s >= 2:
                        evac_o(l, HEADS + s - 2)
                    if s in (2, 3, 4, 5):
                        split_hi(act, l, index["XO0", s - 2])
                for i in range(index["XO1", 0], N1):
                    split_hi(act, l, i)
                square(l, 1)
                for i in range(N1, N1 + 2):
                    split_hi(act, l, i)
                turn_x(l, "XT0c", 0)
                turn_x(l, "XT1c", 1)
                wait_job(l, "RT")
                nc.scalar.activation(logitT[0:NE, :], bank[2 * pair["RT"]][0:NE, 0:T], ACT.Copy).then_inc(job_a.sem, 1)
                wait_job(l, "GT")
                nc.scalar.activation(rt[:, 0, :], bank[2 * pair["GT"]][:, 0:TT * NE], ACT.Exp, scale=-1.0)\
                    .then_inc(job_a.sem, 1)
                for i in range(N1 + 2, N1 + 8):
                    split_hi(act, l, i)
                    if i == N1 + 5:
                        silu_of(l, 0, N1 + 4)
                with act.Fori(0, TURNS) as p:
                    split_hi(act, l, 0, p)
                    split_hi(act, l, 1, p)
                    silu_of(l, 1, p * N_BODY + (N1 + N_PRO))
                    split_hi(act, l, 2, p)
                    split_hi(act, l, 3, p)
                    aT_of(l, p * 2, 0)
                    aT_of(l, p * 2 + 1, 1)
                    for j in range(4, 10):
                        split_hi(act, l, j, p)
                        if j == 5:
                            silu_of(l, 0, p * N_BODY + (N1 + N_PRO + 4))
                    split_hi(act, l, 10, p)
                    split_hi(act, l, 11, p)
                silu_of(l, 1, NSUB - N_EPI)
                aT_of(l, NE - 2, 0)
                aT_of(l, NE - 1, 1)
                for i in range(NSUB - N_EPI, NSUB):
                    split_hi(act, l, i)
                square(l, 2)

        @block.vector
        def _(dve):
            n = [0]

            def then(ins):
                ins.then_inc(const_v, 1)
                n[0] += 1
                dve.wait_ge(const_v, n[0])

            dve.wait_ge(pos_in, 32)
            dve.wait_ge(const_pool, 44)
            TWO_PI = 2 * np.pi
            C1 = 6.28125
            C2 = float(np.float32(np.round((TWO_PI - C1) * 2 ** 17) / 2 ** 17))
            C3 = float(TWO_PI - C1 - C2)
            MAGIC = 1.5 * 2.0 ** 23
            PI_LO = float(np.nextafter(np.float32(np.pi), np.float32(0)))
            a = [ang[:, i, :] for i in range(8)]
            then(nc.vector.tensor_copy(offf[:, 0, 0:TT], pos_i[:, :]))
            for t in range(TT):
                then(nc.vector.tensor_scalar(ang[:, 0, t * 32:(t + 1) * 32], freq[:, t, :], offf[:, 0, t:t + 1], None, ALU.mult))
            then(nc.vector.tensor_scalar(a[1], a[0], 1.0 / TWO_PI, MAGIC, ALU.mult, ALU.add))
            then(nc.vector.tensor_scalar(a[1], a[1], MAGIC, None, ALU.subtract))
            for cc in (C1, C2, C3):
                then(nc.vector.scalar_tensor_tensor(a[0], a[1], -cc, a[0], ALU.mult, ALU.add))
            then(nc.vector.tensor_scalar(a[6], a[0], PI_LO, -PI_LO, ALU.min, ALU.max))
            then(nc.vector.tensor_scalar(a[2], a[0], float(np.pi / 2), None, ALU.add))
            then(nc.vector.tensor_scalar(a[3], a[2], float(np.pi), -TWO_PI, ALU.is_gt, ALU.mult))
            then(nc.vector.tensor_tensor(a[2], a[2], a[3], ALU.add))
            then(nc.vector.tensor_scalar(a[7], a[2], PI_LO, -PI_LO, ALU.min, ALU.max))
            o0, o1, o2 = offf[:, 0, :], offf[:, 1, :], offf[:, 2, :]
            then(nc.vector.tensor_copy(o0, offs[:, :]))
            then(nc.vector.tensor_scalar(o1, o0, 1023.5, None, ALU.is_gt))
            for k, (window, d) in enumerate(DIL):
                if k == 0:
                    then(nc.vector.tensor_scalar(o2, o0, 1024.5 + window, None, ALU.is_lt))
                    then(nc.vector.tensor_tensor(dilcount[:, :], o1, o2, ALU.mult))
                    continue
                then(nc.vector.tensor_scalar(offs2[:, :], offs[:, :], d - 1, None, ALU.bitwise_and))
                then(nc.vector.tensor_copy(o2, offs2[:, :]))
                then(nc.vector.tensor_scalar(o2, o2, 0.0, None, ALU.is_equal))
                then(nc.vector.tensor_tensor(o2, o2, o1, ALU.mult))
                if window < T:
                    raise NotImplementedError
                then(nc.vector.tensor_tensor(dilcount[:, :], dilcount[:, :], o2, ALU.add))
            then(nc.vector.tensor_scalar(dilmask[:, :], dilcount[:, :], 0.5, -BIG, ALU.is_lt, ALU.mult))
            dve.nop().then_inc(angles, 1)
            for k in range(4):
                dve.wait_ge(mem_a, k + 1)
                t, h = k // 2, k % 2
                nc.vector.tensor_tensor(memT_lo[:, 4 * h:4 * h + 4, t * P:(t + 1) * P],
                                        bank[k][:, :].rearrange("p (k m) -> p k m", k=4),
                                        memT_hi[:, 4 * h:4 * h + 4, t * P:(t + 1) * P].bitcast(F32), ALU.subtract)\
                    .then_inc(mem_v, 1)
            dve.wait_ge(const_a, 2)
            dve.nop().then_inc(tables, 1)
            dve.nop().then_inc(lo_ready.sem, RAW)

            def wait_job(l, name):
                dve.wait_ge(*job_done(l, name))

            def turn_x(l, name, t):
                for h, b in enumerate(banks(name)):
                    dve.wait_ge(job_a.sem, job_a.at(l, evac_a[job[name]] - 1 + h))
                    hi = xT_hi[:, 4 * h:4 * h + 4, t * P:(t + 1) * P]
                    nc.vector.tensor_tensor(xT_lo[:, 4 * h:4 * h + 4, t * P:(t + 1) * P],
                                            b[:, :].rearrange("p (k m) -> p k m", k=4), hi.bitcast(F32), ALU.subtract)\
                        .then_inc(job_v.sem, 1)

            def copy_job(l, name, dst, w):
                wait_job(l, name)
                for t, b in enumerate(banks(name)):
                    nc.vector.tensor_copy(dst(t), w(b)).then_inc(job_v.sem, 1)

            def heads_of(b, n_, d):
                return b[:, 0:n_ * d].rearrange("p (h d) -> p h d", h=n_)

            def softmax_max(l, h):
                dve.wait_ge(s_done.sem, s_done.at(l, h + 1))
                if h < HEADS:
                    if h >= 2:
                        dve.wait_ge(pt_done.sem, pt_done.at(l, h - 1))
                    dve.nop().then_inc(paused_v, 1)
                    mask = dilmask if h >= MLA_H + FOX_H else causal
                    scale = float(MLA_D if h < MLA_H else HD) ** -0.5
                    for t in range(TT):
                        sl = slice(0, P) if t == 0 else slice(P, 3 * P)
                        nc.vector.tensor_tensor_reduce(p_sb[:, h % 2, sl], B_S[:, sl], mask[:, P - P * t:2 * P], scale, -3e38,
                                                       ALU.add, ALU.max, mx[:, h, t:t + 1]).then_inc(s_masked.sem, 1)
                    dve.wait_ge(s_masked.sem, s_masked.at(l, 2 * h + 2))
                    nc.vector.tensor_scalar(nmx[:, h, :], mx[:, h, :], -1.0, None, ALU.mult).then_inc(nmx_ready.sem, 1)
                else:
                    nc.vector.tensor_reduce(mx[:, h, :], B_S[:, :].rearrange("p (t n) -> p t n", t=TT), AX, ALU.max)\
                        .then_inc(s_masked.sem, 1)
                    dve.wait_ge(s_masked.sem, s_masked.at(l, HEADS + h + 1))
                    nc.vector.tensor_scalar(nmx[:, h, :], mx[:, h, :], -1.0 / 16.0, None, ALU.mult)\
                        .then_inc(nmx_ready.sem, 1)

            def softmax_norm(l, h):
                dve.wait_ge(e_ready.sem, e_ready.at(l, 2 * h + 2))
                if MLA_H + FOX_H <= h < HEADS:
                    dve.nop().then_inc(paused_v, 1)
                    k = h - MLA_H - FOX_H
                    for t in range(TT):
                        sl = slice(0, P) if t == 0 else slice(P, 3 * P)
                        nc.vector.tensor_tensor_reduce(p_sb[:, h % 2, sl], p_sb[:, h % 2, sl], dilcount[:, P - P * t:2 * P], 1.0, 0.0,
                                                       ALU.mult, ALU.add, sm[:, h, t:t + 1]).then_inc(counted.sem, 1)
                    dve.wait_ge(counted.sem, counted.at(l, 2 * k + 2))
                nc.vector.reciprocal(ri[:, h, :], sm[:, h, :]).then_inc(ri_ready.sem, 1)
                dve.wait_ge(ri_ready.sem, ri_ready.at(l, h + 1))
                for t in range(TT):
                    sl = (slice(0, P) if t == 0 else slice(P, 3 * P)) if h < HEADS else slice(t * T, (t + 1) * T)
                    nc.vector.tensor_scalar(p_sb[:, h % 2, sl], p_sb[:, h % 2, sl], ri[:, h, t:t + 1], None, ALU.mult)\
                        .then_inc(p_ready.sem, 1)

            def evac_pT(l, h):
                dve.wait_ge(pt_done.sem, pt_done.at(l, h + 1))
                if h >= 2:
                    dve.wait_ge(o_done.sem, o_done.at(l, h - 1))
                w = 3 * P if h < HEADS else 4 * P
                nc.vector.tensor_copy(pT[:, h % 2, 0:w], B_PT[:, 0:w]).then_inc(pT_ready.sem, 1)

            def evac_o(l, h):
                n_ = h // 2 if h < HEADS else h - HEADS // 2
                dve.wait_ge(o_hi.sem, o_hi.at(l, n_ + 1))
                if h < HEADS:
                    o, b = slice(h // 2, h // 2 + 1), B_O[:, 0:T].unsqueeze(1)
                else:
                    k = 2 * (h - HEADS)
                    o, b = slice(k, k + 2), B_O[:, :].rearrange("p (c t) -> p c t", c=2)
                nc.vector.tensor_tensor(mixT_lo[:, o, :], b, mixT_hi[:, o, :].bitcast(F32), ALU.subtract)\
                    .then_inc(o_lo.sem, 1)

            def add_job(l, n_, name, h):
                wait_job(l, name)
                for t, b in enumerate(banks(name)):
                    half = xs[:, t, 512 * h:512 * h + 512]
                    nc.vector.scalar_tensor_tensor(half, half, ALPHA, b[:, :], ALU.mult, ALU.add,
                                                   accum_out=st[:, 2 * n_ + t, 2 * h:2 * h + 1])\
                        .then_inc(job_v.sem, 1)

            def means(l, n_, name):
                if name:
                    dve.wait_ge(job_v.sem, job_v.at(l, evac_v[job[name]]))
                else:
                    dve.wait_ge(split_free.sem, split_free.at(l, NSUB))
                    for t in range(TT):
                        for h in range(2):
                            nc.vector.scalar_tensor_tensor(xs[:, t, 512 * h:512 * h + 512],
                                                           xs[:, t, 512 * h:512 * h + 512], ALPHA,
                                                           bank[2 * t + h][:, :], ALU.mult, ALU.add,
                                                           accum_out=st[:, 2 * n_ + t, 2 * h:2 * h + 1])\
                                .then_inc(acc_read.sem, 1)
                    dve.wait_ge(acc_read.sem, acc_read.at(l, 4))
                for t in range(TT):
                    k = 2 * n_ + t
                    nc.vector.tensor_scalar(st[:, k, 0:1], st[:, k, 0:1], st[:, k, 2:3], None, ALU.add)\
                        .then_inc(ln_sum.sem, 1)
                for t in range(TT):
                    k = 2 * n_ + t
                    dve.wait_ge(ln_sum.sem, ln_sum.at(l, k + 1))
                    nc.vector.tensor_scalar(st[:, k, 1:2], st[:, k, 0:1], -1.0 / DM, None, ALU.mult)\
                        .then_inc(ln_nmean.sem, 1)

            def norm_x(l, n_):
                dve.wait_ge(gb_in.sem, gb_in.at(l, 32 * (n_ + 1)))
                for t in range(TT):
                    k = 2 * n_ + t
                    dve.wait_ge(ln_nmean.sem, ln_nmean.at(l, k + 1))
                    dve.wait_ge(ln_sq.sem, ln_sq.at(l, k + 1))
                    nc.vector.scalar_tensor_tensor(xs[:, t, :], xs[:, t, :], st[:, k, 1:2], gb[:, 0, :],
                                                   ALU.add, ALU.mult).then_inc(ln_scaled.sem, 1)
                    dve.wait_ge(ln_scaled.sem, ln_scaled.at(l, k + 1))
                    dve.wait_ge(ln_rstd.sem, ln_rstd.at(l, 2 * k + 2))
                    nc.vector.scalar_tensor_tensor(xs[:, t, :], xs[:, t, :], st[:, k, 3:4], gb[:, 1, :],
                                                   ALU.mult, ALU.add).then_inc(x_ready.sem, 1)

            def router(l):
                q = [0]

                def step(ins):
                    ins.then_inc(route.sem, 1)
                    q[0] += 1
                    dve.wait_ge(route.sem, route.at(l, q[0]))

                R = [rt[:, i, :] for i in range(24)]
                G4 = lambda v: v[:, 0:TT * NG]
                dve.wait_ge(job_a.sem, job_a.at(l, evac_a[job["GT"]]))
                step(nc.vector.tensor_scalar(R[1], R[0], 1.0, None, ALU.add))
                step(nc.vector.reciprocal(R[2], R[1]))
                for t in range(TT):
                    step(nc.vector.tensor_tensor(R[3][:, t * NE:(t + 1) * NE], R[2][:, t * NE:(t + 1) * NE],
                                                 rbias[:, :], ALU.add))
                g = R[3].rearrange("p (g i) -> p g i", i=EPG)
                e0, e1_, e2_, e3_ = (g[:, :, i] for i in range(4))
                M, m, N, n2 = (G4(R[i]) for i in range(4, 8))
                nc.vector.tensor_tensor(M, e0, e1_, ALU.max)
                nc.vector.tensor_tensor(m, e0, e1_, ALU.min)
                nc.vector.tensor_tensor(N, e2_, e3_, ALU.max)
                step(nc.vector.tensor_tensor(n2, e2_, e3_, ALU.min))
                top, s1, s2 = (G4(R[i]) for i in range(8, 11))
                nc.vector.tensor_tensor(top, M, N, ALU.max)
                nc.vector.tensor_tensor(s1, M, N, ALU.min)
                step(nc.vector.tensor_tensor(s2, m, n2, ALU.max))
                step(nc.vector.tensor_tensor(s1, s1, s2, ALU.max))
                step(nc.vector.tensor_tensor(s2, top, s1, ALU.add))

                def first_best(v, n_, dst, cand, scratch, desc):
                    v3 = v.rearrange("p (t n) -> p t n", t=TT)
                    step(nc.vector.tensor_reduce(scratch, v3, AX, ALU.max))
                    for t in range(TT):
                        step(nc.vector.tensor_scalar(cand[:, t * n_:(t + 1) * n_], v[:, t * n_:(t + 1) * n_],
                                                     scratch[:, t:t + 1], None, ALU.is_equal))
                    step(nc.vector.tensor_tensor(cand, cand, desc, ALU.mult))
                    step(nc.vector.tensor_reduce(scratch, cand.rearrange("p (t n) -> p t n", t=TT), AX, ALU.max))
                    for t in range(TT):
                        step(nc.vector.tensor_scalar(dst[:, t * n_:(t + 1) * n_], cand[:, t * n_:(t + 1) * n_],
                                                     scratch[:, t:t + 1], None, ALU.is_equal))

                ing = G4(R[11])
                first_best(s2, NG, ing, G4(R[12]), R[13][:, 0:TT], desc4[:, :])
                b3 = ing.unsqueeze(2).to_broadcast([P, TT * NG, EPG])
                step(nc.vector.tensor_scalar(G4(R[14]), ing, -1.0, BIG, ALU.add, ALU.mult))
                o3 = G4(R[14]).unsqueeze(2).to_broadcast([P, TT * NG, EPG])
                k3 = R[15].rearrange("p (g i) -> p g i", i=EPG)
                step(nc.vector.tensor_tensor(k3, g, b3, ALU.mult))
                step(nc.vector.tensor_tensor(k3, k3, o3, ALU.add))
                first_best(R[15], NE, R[16], R[17], R[13][:, 0:TT], desc16[:, :])
                step(nc.vector.scalar_tensor_tensor(R[18], R[16], -2.0 * BIG, R[15], ALU.mult, ALU.add))
                first_best(R[18], NE, R[19], R[17], R[13][:, 0:TT], desc16[:, :])
                step(nc.vector.tensor_tensor(R[20], R[16], R[19], ALU.add))
                step(nc.vector.tensor_tensor(R[21], R[20], R[2], ALU.mult))
                step(nc.vector.tensor_reduce(R[13][:, 0:TT], R[21].rearrange("p (t n) -> p t n", t=TT), AX, ALU.add))
                step(nc.vector.reciprocal(R[13][:, 2:2 + TT], R[13][:, 0:TT]))
                for t in range(TT):
                    step(nc.vector.tensor_scalar(gates[:, t, :], R[21][:, t * NE:(t + 1) * NE],
                                                 R[13][:, 2 + t:3 + t], None, ALU.mult))
                assert q[0] == route.per, q[0]

            def act_of(l, e, par):
                for t in range(TT):
                    dve.wait_ge(silu_ready.sem, silu_ready.at(l, e * 2 + (t + 1)))
                    nc.vector.scalar_tensor_tensor(act_a[:, par, t, :], silu[:, par, t, :],
                                                   gates[:, t, bass.ds(e, 1)], bank[4 + 2 * par + t][:, DE:2 * DE],
                                                   ALU.mult, ALU.mult).then_inc(a_ready.sem, 1)

            def aT_of(l, e, par):
                dve.wait_ge(aT_a.sem, aT_a.at(l, e + 1))
                nc.vector.tensor_tensor(aT_lo[:, par, :, :], bank[6 + par][:, :].rearrange("p (c t) -> p c t", c=2),
                                        aT_hi[:, par, :, :].bitcast(F32), ALU.subtract).then_inc(aT_v.sem, 1)

            with dve.Fori(0, L) as l:
                for i in range(0, 4):
                    split_lo(dve, l, i)
                turn_x(l, "XT0", 0)
                turn_x(l, "XT1", 1)
                for i in range(4, 8):
                    split_lo(dve, l, i)
                dve.wait_ge(small_in.sem, small_in.at(l, 48))
                dve.wait_ge(rms_step.sem, rms_step.at(l, 2))
                for t, b in enumerate(banks("A")):
                    for g_, (c0, w) in enumerate(((0, QR), (QR, KVR))):
                        nc.vector.scalar_tensor_tensor(lat[:, t, c0:c0 + w], b[:, c0:c0 + w], sm1[:, 2 + g_, t:t + 1],
                                                       gains[:, c0:c0 + w], ALU.mult, ALU.mult).then_inc(job_v.sem, 1)
                z3 = lambda i: fz[:, i, :].rearrange("p (t f) -> p t f", t=TT)
                nc.vector.tensor_tensor(z3(0), kf[:, :, ROPE:], bforget[:, :].unsqueeze(1).to_broadcast([P, TT, FOX_H]),
                                        ALU.add).then_inc(fz_v.sem, 1)
                dve.wait_ge(fz_v.sem, fz_v.at(l, 1))
                nc.vector.scalar_tensor_tensor(fz[:, 1, :], fz[:, 0, :], -1.0, fz[:, 0, :], ALU.mult, ALU.max).then_inc(fz_v.sem, 1)
                for i in range(8, 10):
                    split_lo(dve, l, i)
                dve.wait_ge(fz_a.sem, fz_a.at(l, 2))
                nc.vector.scalar_tensor_tensor(fz[:, 1, :], fz[:, 0, :], 0.0, fz[:, 3, :], ALU.min, ALU.subtract)\
                    .then_inc(fz_v.sem, 1)
                for i in range(10, 12):
                    split_lo(dve, l, i)
                copy_job(l, "FK", lambda t: fk[:, t, :, 0:HD], lambda b: heads_of(b, FOX_H, HD))
                for t, b in enumerate(banks("LT")):
                    dve.wait_ge(job_a.sem, job_a.at(l, evac_a[job["LT"]] - 1 + t))
                    nc.vector.tensor_tensor(latT_lo[:, :, t * P:(t + 1) * P],
                                            b[:, 0:3 * P].rearrange("p (k m) -> p k m", k=3),
                                            latT_hi[:, :, t * P:(t + 1) * P].bitcast(F32), ALU.subtract)\
                        .then_inc(job_v.sem, 1)
                    f = b[:, 3 * P:3 * P + FOX_H].unsqueeze(2)
                    nc.vector.tensor_scalar(fq[:, t, :, HD:HD + 1], f, float(HD) ** 0.5, None, ALU.mult)\
                        .then_inc(job_v.sem, 1)
                    nc.vector.tensor_scalar(fk[:, t, :, HD + 1:HD + 2], f, -float(HD) ** 0.5, None, ALU.mult)\
                        .then_inc(job_v.sem, 1)
                for i in range(12, 18):
                    split_lo(dve, l, i)
                    if i == 15:
                        wait_job(l, "UKV")
                        for t, b in enumerate(banks("UKV")):
                            kv = b[:, :].rearrange("p (h d) -> p h d", h=MLA_H)
                            nc.vector.tensor_copy(mk[:, t, :, 0:HD], kv[:, :, 0:HD]).then_inc(job_v.sem, 1)
                            nc.vector.tensor_copy(mv[:, t, :, :], kv[:, :, HD:2 * HD]).then_inc(job_v.sem, 1)
                split_lo(dve, l, 18)
                done = 19
                for s in range(HEADS + 3):
                    for i in ahead_of[s]:
                        if i >= done:
                            split_lo(dve, l, i)
                            done = i + 1
                    if index["DV", 3] in turns[s]:
                        copy_job(l, "DV", lambda t: dv[:, t, :, :], lambda b: heads_of(b, DIL_H, HD))
                    if index["MV0", 3] in turns[s]:
                        copy_job(l, "MV0", lambda t: vx[:, t, 0:512], lambda b: b[:, :])
                    if 1 <= s <= HEADS:
                        softmax_max(l, s - 1)
                    if 2 <= s <= HEADS + 1:
                        evac_pT(l, s - 2)
                    if s >= 3 and (s - 3) % 2 == 1:
                        evac_o(l, s - 3)
                    if 1 <= s <= HEADS:
                        softmax_norm(l, s - 1)
                for i in range(done, index["XQ0", 0]):
                    split_lo(dve, l, i)
                    if i == index["WO1", 1]:
                        add_job(l, 0, "WO0", 0)
                    if i == index["MV1", 1]:
                        add_job(l, 0, "WO1", 1)
                        means(l, 0, "WO1")
                for i in range(index["XQ0", 0], index["XQ0", 2]):
                    split_lo(dve, l, i)
                norm_x(l, 0)
                copy_job(l, "MV1", lambda t: vx[:, t, 512:1024], lambda b: b[:, :])
                turn_x(l, "XT0b", 0)
                turn_x(l, "XT1b", 1)
                for i in range(index["XQ0", 2], index["XQ1", 3] + 1):
                    split_lo(dve, l, i)
                for s in range(X_H + 2):
                    if s < X_H:
                        softmax_max(l, HEADS + s)
                    if 1 <= s <= X_H:
                        evac_pT(l, HEADS + s - 1)
                    if s < X_H:
                        softmax_norm(l, HEADS + s)
                    if s >= 2:
                        evac_o(l, HEADS + s - 2)
                    if s in (2, 3, 4, 5):
                        split_lo(dve, l, index["XO0", s - 2])
                for i in range(index["XO1", 0], N1):
                    split_lo(dve, l, i)
                    if i == index["XO1", 1]:
                        add_job(l, 1, "XO0", 0)
                add_job(l, 1, "XO1", 1)
                means(l, 1, "XO1")
                for i in range(N1, N1 + 2):
                    split_lo(dve, l, i)
                norm_x(l, 1)
                turn_x(l, "XT0c", 0)
                turn_x(l, "XT1c", 1)
                for i in range(N1 + 2, N1 + 4):
                    split_lo(dve, l, i)
                router(l)
                for i in range(N1 + 4, N1 + 8):
                    split_lo(dve, l, i)
                    if i == N1 + 5:
                        act_of(l, 0, 0)
                with dve.Fori(0, TURNS) as p:
                    split_lo(dve, l, 0, p)
                    split_lo(dve, l, 1, p)
                    act_of(l, p * 2 + 1, 1)
                    split_lo(dve, l, 2, p)
                    split_lo(dve, l, 3, p)
                    aT_of(l, p * 2, 0)
                    aT_of(l, p * 2 + 1, 1)
                    for j in range(4, 10):
                        split_lo(dve, l, j, p)
                        if j == 5:
                            act_of(l, p * 2 + 2, 0)
                    split_lo(dve, l, 10, p)
                    split_lo(dve, l, 11, p)
                act_of(l, NE - 1, 1)
                aT_of(l, NE - 2, 0)
                aT_of(l, NE - 1, 1)
                for i in range(NSUB - N_EPI, NSUB):
                    split_lo(dve, l, i)
                means(l, 2, None)
                norm_x(l, 2)

        @block.tensor
        def _(pe):
            pe.wait_ge(const_pool, 44)
            pe.wait_ge(start_in, 32)
            for n in range(4):
                t, h = n // 2, n % 2
                for k in range(4):
                    f = 4 * h + k
                    ins = nc.tensor.transpose(bank[n][:, k * P:(k + 1) * P], mem_tok[:, t, f * P:(f + 1) * P], ident[:, :])
                ins.then_inc(mem_done, 1)
            pe.nop().then_inc(split_free.sem, SPL)
            pe.nop().then_inc(x_ready.sem, 2)
            pe.wait_ge(mem_v, 4)

            def product(o, lhs, rhs, first, last, shared=False):
                nc.tensor.matmul(o, lhs[0], rhs[0], start=first, stop=False, skip_group_check=shared)
                nc.tensor.matmul(o, lhs[0], rhs[1], start=False, stop=False, skip_group_check=shared)
                return nc.tensor.matmul(o, lhs[1], rhs[0], start=False, stop=last, skip_group_check=shared)

            def ready(l, name):
                n = job[name]
                if jobs[n][1]:
                    pe.wait_ge(job_a.sem, job_a.at(l, evac_a[n]))
                if jobs[n][2]:
                    pe.wait_ge(job_v.sem, job_v.at(l, evac_v[n]))

            def open_job(l, name):
                if job[name] >= 2:
                    ready(l, jobs[job[name] - 2][0])

            def sub_in(l, i, p=None):
                pe.wait_ge(lo_ready.sem, lo_ready.at(l, number(i, p) + 1))
                return w_hi[:, i % SPL, :], w_lo[:, i % SPL, :]

            def rows(l, name, j, xhl, w, chunks=None, per=2):
                if j == 0:
                    open_job(l, name)
                parts = sub_in(l, index[name, j])
                chunks = chunks or KC
                for k in range(per):
                    kc = per * j + k
                    r = tuple(v[:, k * w:(k + 1) * w] for v in parts)
                    for t, b in enumerate(banks(name)):
                        lhs = tuple(v[:, kc, t * P:(t + 1) * P] for v in xhl)
                        ins = product(b[:, 0:w], lhs, r, kc == 0, kc == chunks - 1)
                ins.then_inc(split_free.sem, 1)

            def columns(l, name, j, xhl):
                if j == 0:
                    open_job(l, name)
                parts = sub_in(l, index[name, j])
                for k in range(2):
                    kc = 2 * j + k
                    r = tuple(v[:, kc, :] for v in xhl)
                    for cb in range(4):
                        lhs = tuple(v[:, k * 512 + cb * P:k * 512 + (cb + 1) * P] for v in parts)
                        ins = product(banks(name)[cb // 2][:, (cb % 2) * T:(cb % 2 + 1) * T], lhs, r,
                                      kc == 0 and cb % 2 == 0, kc == KC - 1 and cb % 2 == 1, shared=True)
                ins.then_inc(split_free.sem, 1)

            xT, memT, mixT, latT = (xT_hi, xT_lo), (memT_hi, memT_lo), (mixT_hi, mixT_lo), (latT_hi, latT_lo)
            KINDS = {"MK0": (columns, memT), "MK1": (columns, memT), "XQ0": (columns, xT), "XQ1": (columns, xT),
                     "MV0": (rows, memT, 512), "MV1": (rows, memT, 512), "WO0": (rows, mixT, 512),
                     "WO1": (rows, mixT, 512), "XO0": (rows, mixT, 512), "XO1": (rows, mixT, 512),
                     "A": (rows, xT, A_ALL)}

            def gemm(l, i):
                name, j, _ = stream[i]
                if name in KINDS:
                    f, *args = KINDS[name]
                    f(l, name, j, *args)
                else:
                    rows(l, name, j, xT, cols[name][1])

            def turn_x(l, name, t, count):
                pe.wait_ge(x_ready.sem, x_ready.at(l, count))
                open_job(l, name)
                for f in range(KC):
                    ins = nc.tensor.transpose(banks(name)[f // 4][:, (f % 4) * P:(f % 4 + 1) * P],
                                              xs[:, t, f * P:(f + 1) * P], ident[:, :])
                ins.then_inc(turned.sem, 1)

            def head_qk(l, h):
                if h == 0:
                    ready(l, "UKV")
                    pe.wait_ge(rope_step.sem, rope_step.at(l, 14))
                if h == MLA_H:
                    ready(l, "FQ")
                    ready(l, "FK")
                    pe.wait_ge(aug.sem, aug.at(l, 2))
                if h == MLA_H + FOX_H:
                    pe.wait_ge(rope_step.sem, rope_step.at(l, 26))
                if h:
                    pe.wait_ge(qkT_ready.sem, qkT_ready.at(l, h))
                q, k, g = ((mq, mk, h) if h < MLA_H else (fq, fk, h - MLA_H) if h < MLA_H + FOX_H else
                           (dq, dk, h - MLA_H - FOX_H))
                d = MLA_D if h < MLA_H else FOX_D if h < MLA_H + FOX_H else DIL_D
                if h >= MLA_H + FOX_H:
                    pe.nop().then_inc(paused_t, 1)
                for n, v in enumerate((q, k)):
                    for t in range(TT):
                        c0 = (2 * n + t) * P
                        ins = nc.tensor.transpose(B_QK[0:d, c0:c0 + P], v[:, t, g, :], ident[:, :])
                ins.then_inc(qk_done.sem, 1)

            def head_scores(l, h):
                if h < HEADS:
                    pe.wait_ge(qkT_ready.sem, qkT_ready.at(l, h + 1))
                    if h:
                        pe.wait_ge(s_masked.sem, s_masked.at(l, 2 * h))
                    d = MLA_D if h < MLA_H else FOX_D if h < MLA_H + FOX_H else DIL_D
                    v = qkT[0:d, h % 2, :]
                    nc.tensor.matmul(B_S[:, 0:P], v[:, 0:P], v[:, 2 * P:3 * P], start=True, stop=True)
                    nc.tensor.matmul(B_S[:, P:3 * P], v[:, P:2 * P], v[:, 2 * P:4 * P], start=True, stop=True)\
                        .then_inc(s_done.sem, 1)
                else:
                    pe.wait_ge(e_ready.sem, e_ready.at(l, 2 * h))
                    g = h - HEADS
                    for t in range(TT):
                        for c_ in range(2):
                            ins = nc.tensor.matmul(B_S[:, t * T:(t + 1) * T], qTx[:, 2 * g + c_, t * P:(t + 1) * P],
                                                   kTx[:, 2 * g + c_, :], start=c_ == 0, stop=c_ == 1)
                    ins.then_inc(s_done.sem, 1)

            def head_turn(l, h):
                pe.wait_ge(p_ready.sem, p_ready.at(l, 2 * h + 2))
                if h:
                    pe.wait_ge(pT_ready.sem, pT_ready.at(l, h))
                pr = p_sb[:, h % 2, :]
                if h < HEADS:
                    for k in range(3):
                        ins = nc.tensor.transpose(B_PT[:, k * P:(k + 1) * P], pr[:, k * P:(k + 1) * P], ident[:, :])
                else:
                    for t in range(TT):
                        for c_ in range(2):
                            ins = nc.tensor.transpose(B_PT[:, c_ * T + t * P:c_ * T + (t + 1) * P],
                                                      pr[:, t * T + c_ * P:t * T + (c_ + 1) * P], ident[:, :])
                ins.then_inc(pt_done.sem, 1)

            def head_values(l, h):
                pe.wait_ge(pT_ready.sem, pT_ready.at(l, h + 1))
                if h == MLA_H:
                    ready(l, "FV")
                if h == MLA_H + FOX_H:
                    ready(l, "DV")
                if h < HEADS:
                    if h % 2 == 0 and h:
                        pe.wait_ge(o_lo.sem, o_lo.at(l, h // 2))
                    v, g = ((mv, h) if h < MLA_H else (fv, h - MLA_H) if h < MLA_H + FOX_H else
                            (dv, h - MLA_H - FOX_H))
                    o = B_O[(h % 2) * HD:(h % 2 + 1) * HD, :]
                    nc.tensor.matmul(o[:, 0:T], v[:, 0, g, :], pT[:, h % 2, 0:T], start=True, stop=False)
                    nc.tensor.matmul(o[:, P:T], v[:, 1, g, :], pT[:, h % 2, T:T + P], start=False, stop=True)\
                        .then_inc(o_done.sem, 1)
                else:
                    pe.wait_ge(o_lo.sem, o_lo.at(l, h - HEADS // 2))
                    g = h - HEADS
                    for dblk in range(2):
                        for c_ in range(2):
                            f = 2 * g + dblk
                            ins = nc.tensor.matmul(B_O[:, dblk * T:(dblk + 1) * T], vx[:, c_, f * P:(f + 1) * P],
                                                   pT[:, h % 2, c_ * T:(c_ + 1) * T], start=c_ == 0, stop=c_ == 1)
                    ins.then_inc(o_done.sem, 1)

            def experts_up(l, e, i, par, js, p=None):
                for j in js:
                    parts = sub_in(l, i + j, p)
                    for k in range(2):
                        kc = 2 * j + k
                        r = tuple(v[:, k * 512:(k + 1) * 512] for v in parts)
                        for t in range(TT):
                            lhs = tuple(v[:, kc, t * P:(t + 1) * P] for v in xT)
                            ins = product(bank[4 + 2 * par + t][:, :], lhs, r, kc == 0, kc == KC - 1)
                    ins.then_inc(split_free.sem, 1)

            def turn_a(l, e, par):
                pe.wait_ge(a_ready.sem, a_ready.at(l, e * 2 + 2))
                for c_ in range(2):
                    for t in range(TT):
                        ins = nc.tensor.transpose(bank[6 + par][:, c_ * T + t * P:c_ * T + (t + 1) * P],
                                                  act_a[:, par, t, c_ * P:(c_ + 1) * P], ident[:, :])
                ins.then_inc(at_done.sem, 1)

            def experts_down(l, e, i, par, p=None, last=False):
                pe.wait_ge(aT_v.sem, aT_v.at(l, e + 1))
                for c_ in range(2):
                    parts = sub_in(l, i + c_, p)
                    for t in range(TT):
                        for h in range(2):
                            lhs = (aT_hi[:, par, c_, t * P:(t + 1) * P], aT_lo[:, par, c_, t * P:(t + 1) * P])
                            r = tuple(v[:, 512 * h:512 * (h + 1)] for v in parts)
                            ins = product(bank[2 * t + h][:, :], lhs, r, False, last and c_ == 1)
                    ins.then_inc(split_free.sem, 1)

            with pe.Fori(0, L) as l:
                turn_x(l, "XT0", 0, -1)
                turn_x(l, "XT1", 1, 0)
                ready(l, "XT0")
                ready(l, "XT1")
                for i in range(0, 8):
                    gemm(l, i)
                pe.wait_ge(job_v.sem, job_v.at(l, evac_v[job["A"]]))
                pe.wait_ge(fz_v.sem, fz_v.at(l, 3))
                open_job(l, "FK")
                for i in range(8, 12):
                    gemm(l, i)
                open_job(l, "LT")
                for t, b in enumerate(banks("LT")):
                    for k in range(3):
                        nc.tensor.transpose(b[:, k * P:(k + 1) * P], lat[:, t, k * P:(k + 1) * P], ident[:, :])
                    o = b[:, 3 * P:3 * P + FOX_H]
                    lf = fz[:, 1, :].rearrange("p (t f) -> p t f", t=TT)
                    for s in range(t + 1):
                        ins = nc.tensor.matmul(o, (ones if s < t else upto)[:, :], lf[:, s, :], start=s == 0, stop=s == t)
                ins.then_inc(turned.sem, 1)
                open_job(l, "UQ")
                ready(l, "LT")
                rows(l, "UQ", 0, latT, MLA_H * MLA_D, chunks=2)
                rows(l, "UKV", 0, tuple(v[:, 2:3, :] for v in latT), 512, chunks=1, per=1)
                for j in range(4):
                    gemm(l, index["FV", j])
                for s in range(HEADS + 3):
                    for i in turns[s]:
                        gemm(l, i)
                    if s >= 3:
                        head_values(l, s - 3)
                    if 2 <= s <= HEADS + 1:
                        head_turn(l, s - 2)
                    if 1 <= s <= HEADS:
                        head_scores(l, s - 1)
                    if s < HEADS:
                        head_qk(l, s)
                pe.wait_ge(o_lo.sem, o_lo.at(l, HEADS // 2))
                for i in range(index["WO0", 0], index["MV1", 3] + 1):
                    gemm(l, i)
                turn_x(l, "XT0b", 0, 1)
                turn_x(l, "XT1b", 1, 2)
                ready(l, "XT0b")
                ready(l, "XT1b")
                for j in range(4):
                    gemm(l, index["XQ0", j])
                ready(l, "XQ0")
                ready(l, "MK1")
                for s in range(X_H + 2):
                    for i in xturns[s]:
                        gemm(l, i)
                    if s == 2:
                        ready(l, "XQ1")
                        ready(l, "MV1")
                    if s >= 2:
                        head_values(l, HEADS + s - 2)
                    if 1 <= s <= X_H:
                        head_turn(l, HEADS + s - 1)
                    if s < X_H:
                        head_scores(l, HEADS + s)
                pe.wait_ge(o_lo.sem, o_lo.at(l, HEADS // 2 + X_H))
                for i in range(index["XO0", 0], index["XO1", 3] + 1):
                    gemm(l, i)
                turn_x(l, "XT0c", 0, 3)
                turn_x(l, "XT1c", 1, 4)
                ready(l, "XT0c")
                ready(l, "XT1c")
                open_job(l, "RT")
                for j in range(2):
                    parts = sub_in(l, index["RT", j])
                    for k in range(4):
                        kc = 4 * j + k
                        lhs = tuple(v[:, k * NE:k * NE + P] for v in parts)
                        ins = product(banks("RT")[0][:, 0:T], lhs, tuple(v[:, kc, :] for v in xT), kc == 0, kc == KC - 1)
                    ins.then_inc(split_free.sem, 1)
                open_job(l, "GT")
                ready(l, "RT")
                pe.nop().then_inc(paused_t, 1)
                for t in range(TT):
                    ins = nc.tensor.transpose(banks("GT")[0][:, t * NE:(t + 1) * NE], logitT[0:NE, t * P:(t + 1) * P],
                                              ident[0:NE, 0:NE])
                ins.then_inc(turned.sem, 1)
                ready(l, "GT")
                pe.wait_ge(acc_zero.sem, acc_zero.at(l, 1))
                for b in bank[0:4]:
                    nc.tensor.matmul(b[:, :], zero1[:, 0:P], zero1[:, :], start=True, stop=False)
                experts_up(l, 0, N1, 0, range(4))
                experts_up(l, 1, N1 + 4, 1, range(4))
                with pe.Fori(0, TURNS) as p:
                    pe.wait_ge(a_ready.sem, a_ready.at(l, p * 4 + 2))
                    experts_up(l, p * 2 + 2, 0, 0, (0, 1), p)
                    pe.wait_ge(a_ready.sem, a_ready.at(l, p * 4 + 4))
                    turn_a(l, p * 2, 0)
                    turn_a(l, p * 2 + 1, 1)
                    experts_up(l, p * 2 + 2, 0, 0, (2, 3), p)
                    experts_down(l, p * 2, 4, 0, p)
                    experts_down(l, p * 2 + 1, 6, 1, p)
                    experts_up(l, p * 2 + 3, 8, 1, range(4), p)
                pe.wait_ge(a_ready.sem, a_ready.at(l, 2 * NE))
                turn_a(l, NE - 2, 0)
                turn_a(l, NE - 1, 1)
                experts_down(l, NE - 2, NSUB - 4, 0)
                experts_down(l, NE - 1, NSUB - 2, 1, last=True)


_INS = ["x", "mem", "positions", "w_in", "b_forget", "mla_q_gain", "mla_kv_gain", "mla_w_uq", "mla_w_ukv",
        "w_mix_out", "ln_mix_g", "ln_mix_b", "xattn_w_q", "xattn_w_kv", "xattn_w_o", "ln_mem_g", "ln_mem_b",
        "router_w", "router_bias", "expert_w_gate", "expert_w_up", "expert_w_down", "ln_ffn_g", "ln_ffn_b"]


def kernel(**inputs):
    import concourse.bacc as _bacc
    from concourse.bass_utils import run_bass_kernel_spmd as _run

    nc = _bacc.Bacc("TRN2", target_bir_lowering=False, num_devices=1)
    arrays, args = {}, []
    for name in _INS:
        a = np.ascontiguousarray(inputs[name])
        arrays[f"in_{name}_dram"] = a
        args.append(nc.dram_tensor(f"in_{name}_dram", a.shape, mybir.dt.from_np(a.dtype), kind="ExternalInput").ap())
    out = nc.dram_tensor("out_dram", inputs["x"].shape, F32, kind="ExternalOutput").ap()
    build(nc, *args, out)
    r = _run(nc, [arrays], core_ids=[0])
    return r.results[0]["out_dram"]
```

```python
from contextlib import ExitStack

import numpy as np

import concourse.bass as bass
from concourse import mybir

F32 = mybir.dt.float32
F32R = mybir.dt.float32r
I32 = mybir.dt.int32
ALU = mybir.AluOpType
ACT = mybir.ActivationFunctionType
AX = mybir.AxisListType.X

P = 128
MLA_H, FOX_H, DIL_H, X_H = 4, 6, 6, 4
HD = 64
ROPE = 32
MLA_D, FOX_D, DIL_D = 96, 66, 64
QR, KVR = 256, 128
NE, NG, EPG, DE = 16, 4, 4, 256
DIL = ((128, 1), (512, 4), (2048, 16))
EPS = 1e-5
BIG = 1e30
THETA = 10000.0

RAW = 12
SPL = 4


class Signal:

    def __init__(self, sem, per, ahead=0):
        self.sem, self.per, self.ahead = sem, per, ahead

    def at(self, layer, count):
        return layer * self.per + (self.ahead + count)


def weight_stream():
    subs = []
    for name in ("A", "FQ"):
        subs += [(name, j, 0) for j in range(4)]
    subs += [("FK", j, 0) for j in range(4)]
    subs += [("UQ", 0, 0), ("UKV", 0, 0)]
    for name in ("FV", "DQ", "DK", "DV"):
        subs += [(name, j, 0) for j in range(4)]
    for name in ("MK0", "MK1", "MV0", "WO0", "WO1", "MV1", "XQ0", "XQ1", "XO0", "XO1"):
        subs += [(name, j, 0) for j in range(4)]
    subs += [("RT", j, 0) for j in range(2)]
    return subs


def build(nc, x, mem, positions, w_in, b_forget, mla_q_gain, mla_kv_gain, mla_w_uq, mla_w_ukv, w_mix_out,
          ln_mix_g, ln_mix_b, xattn_w_q, xattn_w_kv, xattn_w_o, ln_mem_g, ln_mem_b, router_w, router_bias,
          expert_w_gate, expert_w_up, expert_w_down, ln_ffn_g, ln_ffn_b, out):
    _, T, DM = x.shape
    L = w_in.shape[0]
    TT = T // P
    KC = DM // P
    assert TT == 2 and KC == 8 and mem.shape[1] == T
    ALPHA = float((2 * L) ** 0.25)
    HEADS = MLA_H + FOX_H + DIL_H

    c = 0
    cols = {}
    for name, width in (("CQ", QR), ("CKV", KVR), ("KR", ROPE), ("FQ", FOX_H * HD), ("FK", FOX_H * HD),
                        ("FV", FOX_H * HD), ("FF", FOX_H), ("DQ", DIL_H * HD), ("DK", DIL_H * HD),
                        ("DV", DIL_H * HD)):
        cols[name] = (c, width)
        c += width
    A_W = QR + KVR + ROPE
    A_ALL = A_W + FOX_H

    stream = weight_stream()
    index = {}
    for i, (name, j, _) in enumerate(stream):
        index[name, j] = i
    N1 = len(stream)
    N_PRO, N_BODY, N_EPI = 10, 24, 14
    TURNS = NG - 1
    NSUB = N1 + N_PRO + TURNS * N_BODY + N_EPI
    assert NSUB % RAW == 0 and N_BODY % RAW == 0 and NSUB % SPL == 0 and N_BODY % SPL == 0

    def width(i):
        name = stream[i][0]
        if name == "A":
            return 2 * A_ALL
        if name in cols:
            return 2 * cols[name][1]
        return {"UQ": 768, "UKV": 512, "RT": 64}.get(name, 1024)

    def brings(i):
        return 32 if i < N1 and stream[i][0] == "A" else 16

    pair_brings = [32] * 4 + [16] * 2
    pro_brings = [32] * 4 + pair_brings
    body_brings = EPG * pair_brings
    epi_brings = 2 * pair_brings + [16] * 2
    landed_value, slot_total = [], [0] * RAW
    for i in range(N1 + N_PRO):
        slot_total[i % RAW] += brings(i) if i < N1 else pro_brings[i - N1]
        landed_value.append(slot_total[i % RAW])
    slot_turn, body_start = [0] * RAW, []
    for j in range(N_BODY):
        slot = (N1 + N_PRO + j) % RAW
        slot_turn[slot] += body_brings[j]
        body_start.append(slot_total[slot] + slot_turn[slot])
    for slot in range(RAW):
        slot_total[slot] += TURNS * slot_turn[slot]
    epi_value = []
    for j in range(N_EPI):
        slot = (NSUB - N_EPI + j) % RAW
        slot_total[slot] += epi_brings[j]
        epi_value.append(slot_total[slot])

    with ExitStack() as ctx:
        base = -(-nc.sbuf_base // 64) * 64
        place = [base]

        def sb(name, shape, dt=F32, at=None):
            size = int(np.prod(shape[1:])) * 4
            size = -(-size // 64) * 64
            if at is None:
                at = place[0]
                place[0] += size
            return nc.alloc_sbuf_tensor_at(name, shape, dt, offset=at), at + size

        raw, _ = sb("raw", [P, RAW, 1024])
        w_hi, _ = sb("w_hi", [P, SPL, 1024], F32R)
        w_lo, _ = sb("w_lo", [P, SPL, 1024], F32R)
        xs, _ = sb("xs", [P, TT, DM])
        xT_at = place[0]
        xT_hi, _ = sb("xT_hi", [P, KC, T], F32R)
        xT_lo, _ = sb("xT_lo", [P, KC, T], F32R)
        memT_hi, _ = sb("memT_hi", [P, KC, T], F32R)
        memT_lo, _ = sb("memT_lo", [P, KC, T], F32R)
        gb, _ = sb("gb", [P, 2, DM])
        ident, _ = sb("ident", [P, P])
        causal, _ = sb("causal", [P, 2 * P])
        dilmask, _ = sb("dilmask", [P, 2 * P])
        dilcount, _ = sb("dilcount", [P, 2 * P])
        upto, _ = sb("upto", [P, P])
        ones, _ = sb("ones", [P, P])
        cosb, _ = sb("cosb", [P, TT, 32])
        sinb, _ = sb("sinb", [P, TT, 32])
        gains, _ = sb("gains", [P, QR + KVR])
        bforget, _ = sb("bforget", [P, FOX_H])
        rbias, _ = sb("rbias", [P, NE])
        mhalf, _ = sb("mhalf", [P, 4])
        nmean, _ = sb("nmean", [P, 1])
        st, _ = sb("st", [P, 8, 4])
        mx, _ = sb("mx", [P, HEADS + X_H, TT])
        nmx, _ = sb("nmx", [P, HEADS + X_H, TT])
        sm, _ = sb("sm", [P, HEADS + X_H, TT])
        sm1, _ = sb("sm1", [P, HEADS, TT])
        ri, _ = sb("ri", [P, HEADS + X_H, TT])
        gates, _ = sb("gates", [P, TT, NE])
        desc16, _ = sb("desc16", [P, TT * NE])
        desc4, _ = sb("desc4", [P, TT * NG])
        iota, _ = sb("iota", [P, P])
        ing, _ = sb("ing", [P, TT * NG])
        g4, _ = sb("g4", [P, TT, EPG])
        posg, _ = sb("posg", [P, TT, NG])
        pos1, _ = sb("pos1", [P, TT])
        gs, _ = sb("gs", [P, NE])
        fl, _ = sb("fl", [P, 2 * NG + 2])
        flag, _ = sb("flag", [1, 2], I32)
        work = place[0]

        mixT_hi, _ = sb("mixT_hi", [P, KC, T], F32R)
        mixT_lo, _ = sb("mixT_lo", [P, KC, T], F32R)
        mq, _ = sb("mq", [P, TT, MLA_H, MLA_D])
        q_work = place[0]
        mk, _ = sb("mk", [P, TT, MLA_H, MLA_D])
        mv, _ = sb("mv", [P, TT, MLA_H, HD])
        fq, _ = sb("fq", [P, TT, FOX_H, FOX_D])
        fk, _ = sb("fk", [P, TT, FOX_H, FOX_D])
        fv, _ = sb("fv", [P, TT, FOX_H, HD])
        dq, _ = sb("dq", [P, TT, DIL_H, HD])
        dk, _ = sb("dk", [P, TT, DIL_H, HD])
        dv, _ = sb("dv", [P, TT, DIL_H, HD])
        kv_work = place[0]
        kTx, _ = sb("kTx", [P, KC, T])
        vx, _ = sb("vx", [P, TT, DM])
        head_work = place[0]
        qkT, _ = sb("qkT", [P, 2, 4 * P])
        p_sb, _ = sb("p_sb", [P, 2, 4 * P])
        pT, _ = sb("pT", [P, 2, 4 * P])
        used = place[0]
        junk, _ = sb("junk", [P, DM], at=head_work)
        lat, _ = sb("lat", [P, TT, QR + KVR], at=head_work)
        latT_hi, e2 = sb("latT_hi", [P, 3, T], F32R, at=kv_work)
        latT_lo, e3 = sb("latT_lo", [P, 3, T], F32R, at=e2)
        rot, e5 = sb("rot", [P, 2, 2, TT * DIL_H * 32], at=kv_work + 8192)
        assert e3 <= kv_work + 8192 and e5 <= head_work
        scaled, e6 = sb("scaled", [P, TT, DM], at=head_work + 4 * DM)
        assert e6 <= used
        kf, _ = sb("kf", [P, TT, ROPE + FOX_H])
        fz, _ = sb("fz", [P, 4, TT * FOX_H])
        qTx, e4 = sb("qTx", [P, KC, T], at=q_work)
        xg, m0 = sb("xg", [P, KC, NG, P], at=work)
        cur_hi, m1 = sb("cur_hi", [P, KC, P], F32R, at=m0)
        cur_lo, m2 = sb("cur_lo", [P, KC, P], F32R, at=m1)
        y_hi, m3 = sb("y_hi", [P, NG, DM], F32R, at=m2)
        y_lo, m4 = sb("y_lo", [P, NG, DM], F32R, at=m3)
        sel, m5 = sb("sel", [P, TT, NG * P], F32R, at=m4)
        assert m5 <= used
        rt, m6 = sb("rt", [P, 24, TT * NE], at=m2)
        logitT, m7 = sb("logitT", [P, T], at=m6)
        xs_hi, _ = sb("xs_hi", [P, TT, DM], F32R, at=xT_at)
        xs_lo, xT_end = sb("xs_lo", [P, TT, DM], F32R, at=xT_at + 4 * TT * DM)
        selT, m1a = sb("selT", [P, NG, T], F32R, at=xT_at)
        act_a, m2a = sb("act_a", [P, 2, DE], at=m1a)
        silu, m3a = sb("silu", [P, 2, DE], at=m2a)
        aT_hi, m4a = sb("aT_hi", [P, 2, 2, P], F32R, at=m3a)
        aT_lo, m5a = sb("aT_lo", [P, 2, 2, P], F32R, at=m4a)
        assert m5a <= xT_end
        ov_up, o1 = sb("ov_up", [P, KC, 2 * DE], at=work)
        ov_down, o2 = sb("ov_down", [P, 2, DM], at=o1)
        ov_x, o3 = sb("ov_x", [P, KC, P], at=m5)
        ov_y, o4 = sb("ov_y", [P, DM], at=o3)
        ov_sel, o5 = sb("ov_sel", [P, TT, P], at=m4)
        ov_selT, o6 = sb("ov_selT", [P, T], at=o5)
        ov_aT, o7 = sb("ov_aT", [P, 2, P], at=o6)
        ov_gs, o8 = sb("ov_gs", [P, EPG], at=o7)
        assert o2 <= m2 and o4 <= used and o8 <= m5
        mem_tok, _ = sb("mem_tok", [P, TT, DM], at=work)
        pos_i, b1 = sb("pos_i", [P, TT], I32, at=work + 8192)
        ang, b2 = sb("ang", [P, 8, TT * 32], at=b1)
        freq, b3 = sb("freq", [P, TT, 32], at=b2)
        offs, b4 = sb("offs", [P, 2 * P], I32, at=b3)
        offs2, b5 = sb("offs2", [P, 2, 2 * P], I32, at=b4)
        offf, b6 = sb("offf", [P, 3, 2 * P], at=b5)
        assert b6 <= used and place[0] <= nc.sbuf_usable_end, (place[0], nc.sbuf_usable_end)

        bank = [ctx.enter_context(nc.psum_tensor(f"bank{i}", [P, 512], F32)) for i in range(8)]
        B_QK, B_S, B_PT, B_O = bank[4], bank[5], bank[6], bank[7]

        def sem(name):
            return ctx.enter_context(nc.semaphore(name))

        def signal(name, per, ahead=0):
            return Signal(sem(name), per, ahead)

        jobs = [("XT0", 2, 2), ("XT1", 2, 2), ("A", 6, 4), ("FQ", 2, 0), ("FK", 0, 2), ("LT", 2, 6),
                ("UQ", 2, 0), ("UKV", 0, 4), ("FV", 2, 0), ("DQ", 2, 0), ("DK", 2, 0), ("DV", 0, 2),
                ("MK0", 2, 0), ("MK1", 2, 0), ("MV0", 0, 2), ("WO0", 0, 2), ("WO1", 0, 2), ("MV1", 0, 2),
                ("XT0b", 2, 2), ("XT1b", 2, 2), ("XQ0", 2, 0), ("XQ1", 2, 0), ("XO0", 0, 2), ("XO1", 0, 2),
                ("XT0c", 2, 2), ("XT1c", 2, 2), ("RT", 1, 0), ("GT", 1, 0)]
        job = {name: n for n, (name, _, _) in enumerate(jobs)}
        pair = {name: n % 2 for n, (name, _, _) in enumerate(jobs)}
        evac_a = np.cumsum([a for _, a, _ in jobs]).tolist()
        evac_v = np.cumsum([v for _, _, v in jobs]).tolist()

        XG_BANK = (0, 1, 6, 7, 3, 2, 6, 7)

        turning = ["XT0", "XT1", "LT", "XT0b", "XT1b", "XT0c", "XT1c", "GT"]
        last_sub = {name: i for (name, _), i in index.items()}

        def job_done(l, name):
            if name in turning:
                return turned.sem, turned.at(l, turning.index(name) + 1)
            return split_free.sem, split_free.at(l, last_sub[name] + 1)

        def banks(name):
            return [bank[2 * pair[name]], bank[2 * pair[name] + 1]]

        raw_in = [Signal(sem(f"raw_in{i}"), slot_total[i]) for i in range(RAW)]
        hi_ready = signal("hi_ready", NSUB)
        lo_ready = signal("lo_ready", NSUB, RAW)
        split_free = signal("split_free", NSUB, SPL)
        turned = signal("turned", 8)
        job_a = signal("job_a", evac_a[-1])
        job_v = signal("job_v", evac_v[-1])
        x_ready = signal("x_ready", 6, 2)
        ln_nmean = signal("ln_nmean", 6)
        ln_sq = signal("ln_sq", 6)
        ln_rstd = signal("ln_rstd", 12)
        ln_scaled = signal("ln_scaled", 6)
        gb_in = signal("gb_in", 96)
        small_in = signal("small_in", 48)
        qk_done = signal("qk_done", HEADS)
        qkT_ready = signal("qkT_ready", HEADS)
        s_done = signal("s_done", HEADS + X_H)
        s_masked = signal("s_masked", 2 * HEADS + X_H)
        nmx_ready = signal("nmx_ready", HEADS + X_H)
        e_ready = signal("e_ready", 2 * (HEADS + X_H))
        counted = signal("counted", 2 * DIL_H)
        ri_ready = signal("ri_ready", HEADS + X_H)
        p_ready = signal("p_ready", 2 * (HEADS + X_H))
        pt_done = signal("pt_done", HEADS + X_H)
        pT_ready = signal("pT_ready", HEADS + X_H)
        acc_read = signal("acc_read", 4)
        o_done = signal("o_done", HEADS + X_H)
        o_hi = signal("o_hi", HEADS // 2 + X_H)
        o_lo = signal("o_lo", HEADS // 2 + X_H)
        rms_step = signal("rms_step", 2)
        fz_v = signal("fz_v", 3)
        fz_a = signal("fz_a", 2)
        aug = signal("aug", 2)
        rope_step = signal("rope_step", 26)
        route = signal("route", 47)
        group_at = 15
        xs_a = signal("xs_a", TT)
        xs_p = signal("xs_p", TT)
        ranked = signal("ranked", 1)
        sel_ready = signal("sel_ready", TT)
        gs_done = signal("gs_done", 1)
        gs_ready = signal("gs_ready", 1)
        xg_done = signal("xg_done", KC)
        xg_a = signal("xg_a", KC // 2)
        xg_v = signal("xg_v", KC // 2)
        cur_a = signal("cur_a", 2 * NG)
        cur_v = signal("cur_v", 2 * NG)
        selT_done = signal("selT_done", 1)
        selT_a = signal("selT_a", 2)
        silu_ready = signal("silu_ready", NE)
        a_ready = signal("a_ready", NE)
        at_done = signal("at_done", NE)
        aT_a = signal("aT_a", NE)
        aT_v = signal("aT_v", NE)
        y_a = signal("y_a", 2 * NG)
        y_v = signal("y_v", 2 * NG)
        summed = signal("summed", 2)
        flag_ready = signal("flag_ready", 3)
        ov_in = signal("ov_in", 48 * EPG)
        ov_picked = signal("ov_picked", 1 + TT)
        ov_gathered = signal("ov_gathered", 1)
        ov_kept = signal("ov_kept", 5)
        ov_upped = signal("ov_upped", EPG)
        ov_silu = signal("ov_silu", EPG)
        ov_act = signal("ov_act", EPG)
        ov_turned = signal("ov_turned", EPG)
        ov_aT_in = signal("ov_aT_in", EPG)
        ov_used = signal("ov_used", EPG, 1)
        ov_y_in = signal("ov_y_in", 1 + 2 * EPG)
        start_in = sem("start_in")
        warmed = sem("warmed")
        strides = sem("strides")
        paused_v, paused_p, paused_t = sem("paused_v"), sem("paused_p"), sem("paused_t")
        paused_a = sem("paused_a")
        mem_in = sem("mem_in")
        pos_in = sem("pos_in")
        bias_in = sem("bias_in")
        const_pool = sem("const_pool")
        const_v = sem("const_v")
        const_a = sem("const_a")
        angles = sem("angles")
        tables = sem("tables")
        mem_done = sem("mem_done")
        mem_a = sem("mem_a")
        mem_v = sem("mem_v")
        out_sent = sem("out_sent")

        feat = lambda w: w.rearrange("(k p) n -> p k n", p=P)

        slots = [2] * 3 + [1] * 7 + [2] * 6 + [1] * 3
        fill = [index["FV", 0] + i for i in range(28)]
        assert sum(slots) == len(fill)
        turns, k = [], 0
        for n in slots:
            turns.append(fill[k:k + n])
            k += n
        assert len(turns) == HEADS + 3
        xturns = [[index["XQ1", 0], index["XQ1", 1]], [index["XQ1", 2], index["XQ1", 3]], [],
                  [index["XO0", 0]], [index["XO0", 1]], [index["XO0", 2]]]
        assert len(xturns) == X_H + 2

        def score_bank(h):
            return B_QK if h >= HEADS and (h - HEADS) % 2 else B_S

        ahead_of = turns[1:] + [[index["WO0", 0], index["WO0", 1]]]

        block = ctx.enter_context(nc.Block())

        @block.sync
        def _(sp):
            sp.dma_start(pos_i[:, :], positions[0].rearrange("(t p) -> p t", p=P),
                         allow_slow_non_contiguous=True).then_inc(pos_in, 16)
            sp.dma_start(mem_tok[:, :, :], mem[0].rearrange("(t p) d -> p t d", p=P)).then_inc(mem_in, 16)
            sp.dma_start(xs[:, :, :], x[0].rearrange("(t p) d -> p t d", p=P)).then_inc(start_in, 16)

            def load(l, i, slot, pieces):
                sp.wait_ge(lo_ready.sem, lo_ready.at(l, i - RAW + 1))
                for dst, src in pieces:
                    sp.dma_start(dst, src).then_inc(raw_in[slot].sem, 16)

            def straight(l, i):
                name, j, _ = stream[i]
                slot = i % RAW
                row = raw[:, slot, 0:width(i)]
                if name == "A":
                    r = row.rearrange("p (k n) -> p k n", k=2)
                    w = feat(w_in[l])[:, 2 * j:2 * j + 2, :]
                    f0 = cols["FF"][0]
                    return [(r[:, :, 0:A_W], w[:, :, 0:A_W]), (r[:, :, A_W:A_ALL], w[:, :, f0:f0 + FOX_H])]
                if name in cols:
                    c0, n = cols[name]
                    return [(row.rearrange("p (k n) -> p k n", k=2), feat(w_in[l])[:, 2 * j:2 * j + 2, c0:c0 + n])]
                if name == "UQ":
                    return [(row.rearrange("p (k n) -> p k n", k=2), feat(mla_w_uq[l]))]
                if name == "UKV":
                    return [(row, mla_w_ukv[l])]
                if name == "RT":
                    return [(row.rearrange("p (k n) -> p k n", k=4), feat(router_w)[:, 4 * j:4 * j + 4, :])]
                src, c0 = {"MK0": (xattn_w_kv, 0), "MK1": (xattn_w_kv, 512), "MV0": (xattn_w_kv, 1024),
                           "MV1": (xattn_w_kv, 1536), "WO0": (w_mix_out, 0), "WO1": (w_mix_out, 512),
                           "XQ0": (xattn_w_q, 0), "XQ1": (xattn_w_q, 512), "XO0": (xattn_w_o, 0),
                           "XO1": (xattn_w_o, 512)}[name]
                return [(row.rearrange("p (k n) -> p k n", k=2), feat(src[l])[:, 2 * j:2 * j + 2, c0:c0 + 512])]

            def up(l, e, i, slot0):
                for j in range(4):
                    slot = (slot0 + j) % RAW
                    r = raw[:, slot, :].rearrange("p (k g n) -> p k g n", k=2, g=2)
                    load(l, i + j, slot, [(r[:, :, g, :], feat(w[l][e])[:, 2 * j:2 * j + 2, :])
                                          for g, w in enumerate((expert_w_gate, expert_w_up))])

            def down(l, e, i, slot0):
                for j in range(2):
                    slot = (slot0 + j) % RAW
                    load(l, i + j, slot, [(raw[:, slot, :], expert_w_down[l][e][j * P:(j + 1) * P, :])])

            with sp.Fori(0, L) as l:
                for i in range(N1):
                    load(l, i, i % RAW, straight(l, i))
                up(l, 0, N1, N1)
                up(l, 1, N1 + 4, N1 + 4)
                down(l, 0, N1 + 8, N1 + 8)
                with sp.Fori(0, TURNS) as p:
                    for j in range(EPG):
                        i = p * N_BODY + (N1 + N_PRO + 6 * j)
                        e = p * EPG + (j + 1)
                        up(l, e + 1, i, N1 + N_PRO + 6 * j)
                        down(l, e, i + 4, N1 + N_PRO + 6 * j + 4)
                first = NSUB - N_EPI
                for j in range(2):
                    up(l, NE - 2 + j, first + 6 * j, first + 6 * j)
                    down(l, NE - 3 + j, first + 6 * j + 4, first + 6 * j + 4)
                down(l, NE - 1, NSUB - 2, NSUB - 2)
            sp.wait_ge(x_ready.sem, x_ready.at(L - 1, 6))
            sp.dma_start(out[0].rearrange("(t p) d -> p t d", p=P), xs[:, :, :]).then_inc(out_sent, 16)
            sp.wait_ge(out_sent, 16)

        def where(l, i, p=None):
            if p is not None:
                slot = (N1 + N_PRO + i) % RAW
                return slot, raw_in[slot].sem, p * slot_turn[slot] + raw_in[slot].at(l, body_start[i])
            slot = i % RAW
            if i >= NSUB - N_EPI:
                return slot, raw_in[slot].sem, raw_in[slot].at(l, epi_value[i - (NSUB - N_EPI)])
            return slot, raw_in[slot].sem, raw_in[slot].at(l, landed_value[i])

        def number(i, p):
            return i if p is None else p * N_BODY + (N1 + N_PRO + i)

        def split_slot(i, p):
            return (i if p is None else N1 + N_PRO + i) % SPL

        def split_hi(act, l, i, p=None):
            slot, landed, value = where(l, i, p)
            n, w = number(i, p), (width(i) if p is None and i < N1 else 1024)
            act.wait_ge(landed, value)
            act.wait_ge(split_free.sem, split_free.at(l, n - SPL + 1))
            nc.scalar.activation(w_hi[:, split_slot(i, p), 0:w], raw[:, slot, 0:w], ACT.Copy).then_inc(hi_ready.sem, 1)

        def split_lo(dve, l, i, p=None):
            slot, landed, value = where(l, i, p)
            n, w = number(i, p), (width(i) if p is None and i < N1 else 1024)
            dve.wait_ge(hi_ready.sem, hi_ready.at(l, n + 1))
            nc.vector.tensor_tensor(w_lo[:, split_slot(i, p), 0:w], raw[:, slot, 0:w],
                                    w_hi[:, split_slot(i, p), 0:w].bitcast(F32), ALU.subtract).then_inc(lo_ready.sem, 1)

        def overflow(engine, l, paused):
            engine.wait_ge(flag_ready.sem, flag_ready.at(l, 3))
            engine.nop().then_inc(paused, 1)
            return engine.value_load(flag[0:1, 0:1], min_val=0, max_val=1)

        @block.gpsimd
        def _(pool):
            pool.dma_start(rbias[:, :], router_bias.rearrange("(a n) -> a n", a=1).to_broadcast([P, NE])).then_inc(bias_in, 16)
            inv = (np.float32(THETA) ** (-np.arange(32, dtype=np.float32) / np.float32(32))).astype(np.float32)
            for i in range(32):
                nc.gpsimd.memset(freq[:, :, i:i + 1], float(inv[i])).then_inc(const_pool, 1)
            nc.gpsimd.memset(ident[:, :], 0.0).then_inc(const_pool, 1)
            nc.gpsimd.memset(causal[:, :], 0.0).then_inc(const_pool, 1)
            nc.gpsimd.memset(upto[:, :], 1.0).then_inc(const_pool, 1)
            nc.gpsimd.memset(ones[:, :], 1.0).then_inc(const_pool, 1)
            nc.gpsimd.memset(mhalf[:, :], -0.5).then_inc(const_pool, 1)
            nc.gpsimd.memset(nmean[:, :], -1.0 / DM).then_inc(const_pool, 1)
            nc.gpsimd.iota(iota[:, :], pattern=[[1, P]], base=0, channel_multiplier=0,
                           allow_small_or_imprecise_dtypes=True).then_inc(const_pool, 1)
            pool.wait_ge(const_pool, 39)
            nc.gpsimd.affine_select(out=ident[:, :], in_=ident[:, :], compare_op=ALU.not_equal, fill=1.0, base=0,
                                    pattern=[[-1, P]], channel_multiplier=1).then_inc(const_pool, 1)
            nc.gpsimd.affine_select(out=upto[:, :], in_=upto[:, :], compare_op=ALU.is_ge, fill=0.0, base=0,
                                    pattern=[[1, P]], channel_multiplier=-1).then_inc(const_pool, 1)
            nc.gpsimd.affine_select(out=causal[:, :], in_=causal[:, :], compare_op=ALU.is_ge, fill=-BIG,
                                    base=P, pattern=[[-1, 2 * P]], channel_multiplier=1).then_inc(const_pool, 1)
            nc.gpsimd.iota(offs[:, :], pattern=[[-1, 2 * P]], base=1024 + P, channel_multiplier=1)\
                .then_inc(const_pool, 1)
            nc.gpsimd.iota(desc16[:, :], pattern=[[0, TT], [-1, NE]], base=NE, channel_multiplier=0,
                           allow_small_or_imprecise_dtypes=True).then_inc(const_pool, 1)
            nc.gpsimd.iota(desc4[:, :], pattern=[[0, TT], [-1, NG]], base=NG, channel_multiplier=0,
                           allow_small_or_imprecise_dtypes=True).then_inc(const_pool, 1)

            steps = [45]

            def step(ins):
                ins.then_inc(const_pool, 1)
                steps[0] += 1
                pool.wait_ge(const_pool, steps[0])

            pool.wait_ge(const_pool, 45)
            o0, o1, o2 = offf[:, 0, :], offf[:, 1, :], offf[:, 2, :]
            step(nc.gpsimd.tensor_copy(o0, offs[:, :]))
            step(nc.gpsimd.tensor_scalar(o1, o0, 1023.5, None, ALU.is_gt))
            for k, (window, d) in enumerate(DIL):
                if k == 0:
                    step(nc.gpsimd.tensor_scalar(o2, o0, 1024.5 + window, None, ALU.is_lt))
                    step(nc.gpsimd.tensor_tensor(dilcount[:, :], o1, o2, ALU.mult))
                    continue
                pool.wait_ge(strides, k)
                step(nc.gpsimd.tensor_copy(o2, offs2[:, k - 1, :]))
                step(nc.gpsimd.tensor_scalar(o2, o2, 0.0, None, ALU.is_equal))
                step(nc.gpsimd.tensor_tensor(o2, o2, o1, ALU.mult))
                if window < T:
                    raise NotImplementedError
                step(nc.gpsimd.tensor_tensor(dilcount[:, :], dilcount[:, :], o2, ALU.add))
            step(nc.gpsimd.tensor_scalar(dilmask[:, :], dilcount[:, :], 0.5, -BIG, ALU.is_lt, ALU.mult))
            def rotate(l, dst, src, n_heads, half, step, n0):
                shape = [P, TT, n_heads, half]
                c_ = cosb[:, :, 0:32:step].unsqueeze(2).to_broadcast(shape)
                s_ = sinb[:, :, 0:32:step].unsqueeze(2).to_broadcast(shape)
                x1, x2 = src[:, :, :, 0:half], src[:, :, :, half:2 * half]
                n = TT * n_heads * half
                t = [rot[:, i, j, 0:n].rearrange("p (t h d) -> p t h d", t=TT, h=n_heads) for i in range(2) for j in range(2)]
                if n0:
                    pool.wait_ge(rope_step.sem, rope_step.at(l, n0))
                nc.gpsimd.tensor_tensor(t[0], x1, c_, ALU.mult).then_inc(rope_step.sem, 1)
                nc.gpsimd.tensor_tensor(t[1], x2, s_, ALU.mult).then_inc(rope_step.sem, 1)
                nc.gpsimd.tensor_tensor(t[2], x1, s_, ALU.mult).then_inc(rope_step.sem, 1)
                nc.gpsimd.tensor_tensor(t[3], x2, c_, ALU.mult).then_inc(rope_step.sem, 1)
                pool.wait_ge(rope_step.sem, rope_step.at(l, n0 + 4))
                nc.gpsimd.tensor_tensor(dst[:, :, :, 0:half], t[0], t[1], ALU.subtract).then_inc(rope_step.sem, 1)
                nc.gpsimd.tensor_tensor(dst[:, :, :, half:2 * half], t[2], t[3], ALU.add).then_inc(rope_step.sem, 1)

            def norm(l, n, g_dram, b_dram):
                pool.wait_ge(x_ready.sem, x_ready.at(l, 2 * n))
                pool.nop().then_inc(paused_p, 1)
                for r, d in enumerate((g_dram, b_dram)):
                    pool.dma_start(gb[:, r, :], d[l].rearrange("(a n) -> a n", a=1).to_broadcast([P, DM]))\
                        .then_inc(gb_in.sem, 16)

            def deviation(l, n):
                for t in range(TT):
                    k = 2 * n + t
                    pool.wait_ge(ln_sq.sem, ln_sq.at(l, k + 1))
                    pool.nop().then_inc(paused_p, 1)
                    nc.gpsimd.tensor_scalar(st[:, k, 2:3], st[:, k, 2:3], 1.0 / DM, EPS, ALU.mult, ALU.add)\
                        .then_inc(ln_rstd.sem, 1)
                    pool.wait_ge(ln_rstd.sem, ln_rstd.at(l, 2 * k + 1))
                    nc.gpsimd.tensor_tensor(st[:, k, 3:4], st[:, k, 2:3], mhalf[:, 0:1], ALU.pow)\
                        .then_inc(ln_rstd.sem, 1)

            pool.wait_ge(const_a, 2)
            pool.wait_ge(tables, 1)
            with pool.Fori(0, L) as l:
                norm(l, 0, ln_mix_g, ln_mix_b)
                pool.dma_start(gains[:, 0:QR], mla_q_gain[l].rearrange("(a n) -> a n", a=1).to_broadcast([P, QR]))\
                    .then_inc(small_in.sem, 16)
                pool.dma_start(gains[:, QR:QR + KVR],
                               mla_kv_gain[l].rearrange("(a n) -> a n", a=1).to_broadcast([P, KVR]))\
                    .then_inc(small_in.sem, 16)
                pool.dma_start(bforget[:, :], b_forget[l].rearrange("(a n) -> a n", a=1).to_broadcast([P, FOX_H]))\
                    .then_inc(small_in.sem, 16)
                nc.gpsimd.memset(fq[:, :, :, HD + 1:HD + 2], 1.0).then_inc(aug.sem, 1)
                nc.gpsimd.memset(fk[:, :, :, HD:HD + 1], 1.0).then_inc(aug.sem, 1)
                pool.wait_ge(job_a.sem, job_a.at(l, evac_a[job["A"]]))
                pool.nop().then_inc(paused_p, 1)
                sq = sm1[:, 0:2, :]
                nc.gpsimd.tensor_scalar(sq, sq, 1.0, EPS, ALU.mult, ALU.add).then_inc(rms_step.sem, 1)
                pool.wait_ge(rms_step.sem, rms_step.at(l, 1))
                nc.gpsimd.tensor_tensor(sm1[:, 2:4, :], sq, mhalf[:, :].rearrange("p (a b) -> p a b", a=2), ALU.pow)\
                    .then_inc(rms_step.sem, 1)
                kr = kf[:, :, 0:ROPE].unsqueeze(2)
                rotate(l, kr, kr, 1, 16, 2, 0)
                pool.wait_ge(job_a.sem, job_a.at(l, evac_a[job["UQ"]]))
                rotate(l, mq[:, :, :, HD:HD + ROPE], mq[:, :, :, HD:HD + ROPE], MLA_H, 16, 2, 6)
                for t in range(TT):
                    nc.gpsimd.tensor_copy(mk[:, t, :, HD:HD + ROPE],
                                          kf[:, t, 0:ROPE].unsqueeze(1).to_broadcast([P, MLA_H, ROPE]))\
                        .then_inc(rope_step.sem, 1)
                for n, (name, q) in enumerate((("DQ", dq), ("DK", dk))):
                    pool.wait_ge(job_a.sem, job_a.at(l, evac_a[job[name]]))
                    rotate(l, q[:, :, :, :], q[:, :, :, :], DIL_H, 32, 1, 14 + 6 * n)
                deviation(l, 0)
                norm(l, 1, ln_mem_g, ln_mem_b)
                deviation(l, 1)
                for t in range(TT):
                    pool.wait_ge(xs_a.sem, xs_a.at(l, t + 1))
                    nc.gpsimd.tensor_tensor(xs_lo[:, t, :], xs[:, t, :], xs_hi[:, t, :].bitcast(F32), ALU.subtract)\
                        .then_inc(xs_p.sem, 1)
                norm(l, 2, ln_ffn_g, ln_ffn_b)
                over = overflow(pool, l, paused_p)
                which = pool.value_load(flag[0:1, 1:2], min_val=0, max_val=NG - 1)
                with pool.If(over > 0):
                    pool.wait_ge(split_free.sem, split_free.at(l, NSUB))
                    pool.nop().then_inc(paused_p, 1)
                    with pool.Fori(0, EPG) as e:
                        pool.wait_ge(ov_used.sem, ov_used.at(l, e))
                        pool.nop().then_inc(paused_p, 1)
                        for g, w in enumerate((expert_w_gate, expert_w_up)):
                            pool.dma_start(ov_up[:, :, g * DE:(g + 1) * DE], feat(w[l].rearrange("(g e) k n -> g e k n", g=NG)[which][e]))\
                                .then_inc(ov_in.sem, 16)
                        pool.dma_start(ov_down[:, :, :], feat(expert_w_down[l].rearrange("(g e) k n -> g e k n", g=NG)[which][e])).then_inc(ov_in.sem, 16)
                with pool.If(over < 1):
                    pool.nop().then_inc(ov_in.sem, ov_in.per)
                deviation(l, 2)

        @block.scalar
        def _(act):
            act.wait_ge(angles, 1)
            nc.scalar.activation(sinb[:, :, :].rearrange("p t d -> p (t d)"), ang[:, 6, :], ACT.Sin).then_inc(const_a, 1)
            nc.scalar.activation(cosb[:, :, :].rearrange("p t d -> p (t d)"), ang[:, 7, :], ACT.Sin).then_inc(const_a, 1)
            for n in range(4):
                act.wait_ge(mem_done, n + 1)
                t, h = n // 2, n % 2
                nc.scalar.activation(memT_hi[:, 4 * h:4 * h + 4, t * P:(t + 1) * P],
                                     bank[4 + n][:, :].rearrange("p (k m) -> p k m", k=4), ACT.Copy).then_inc(mem_a, 1)

            def wait_job(l, name):
                act.wait_ge(*job_done(l, name))

            def turn_x(l, name, t):
                wait_job(l, name)
                for h, b in enumerate(banks(name)):
                    nc.scalar.activation(xT_hi[:, 4 * h:4 * h + 4, t * P:(t + 1) * P],
                                         b[:, :].rearrange("p (k m) -> p k m", k=4), ACT.Copy).then_inc(job_a.sem, 1)

            def copy_job(l, name, dst, w):
                wait_job(l, name)
                for t, b in enumerate(banks(name)):
                    nc.scalar.activation(dst(t), w(b), ACT.Copy).then_inc(job_a.sem, 1)

            def heads_of(b, n, d):
                return b[:, 0:n * d].rearrange("p (h d) -> p h d", h=n)

            def evac_qk(l, h):
                act.wait_ge(qk_done.sem, qk_done.at(l, h + 1))
                if h >= 2:
                    act.wait_ge(s_done.sem, s_done.at(l, h - 1))
                d = MLA_D if h < MLA_H else FOX_D if h < MLA_H + FOX_H else DIL_D
                nc.scalar.activation(qkT[0:d, h % 2, :], B_QK[0:d, :], ACT.Copy).then_inc(qkT_ready.sem, 1)

            def exps(l, h):
                act.wait_ge(nmx_ready.sem, nmx_ready.at(l, h + 1))
                if h >= 2:
                    act.wait_ge(pt_done.sem, pt_done.at(l, h - 1))
                for t in range(TT):
                    if h < HEADS:
                        sl = slice(0, P) if t == 0 else slice(P, 3 * P)
                        src, scale = p_sb[:, h % 2, sl], 1.0
                    else:
                        sl = slice(t * T, (t + 1) * T)
                        src, scale = score_bank(h)[:, sl], 1.0 / 16.0
                    acc = sm1 if MLA_H + FOX_H <= h < HEADS else sm
                    nc.scalar.activation(p_sb[:, h % 2, sl], src, ACT.Exp, bias=nmx[:, h, t:t + 1], scale=scale,
                                         accum_out=acc[:, h, t:t + 1]).then_inc(e_ready.sem, 1)

            def evac_o(l, h):
                if h < HEADS:
                    n = h // 2
                    act.wait_ge(o_done.sem, o_done.at(l, h + 1))
                    nc.scalar.activation(mixT_hi[:, n, :], B_O[:, 0:T], ACT.Copy).then_inc(o_hi.sem, 1)
                else:
                    n = h - HEADS
                    act.wait_ge(o_done.sem, o_done.at(l, h + 1))
                    nc.scalar.activation(mixT_hi[:, 2 * n:2 * n + 2, :],
                                         B_O[:, :].rearrange("p (c t) -> p c t", c=2), ACT.Copy).then_inc(o_hi.sem, 1)

            def square(l, n):
                for t in range(TT):
                    k = 2 * n + t
                    act.wait_ge(ln_nmean.sem, ln_nmean.at(l, k + 1))
                    if k:
                        act.wait_ge(ln_sq.sem, ln_sq.at(l, k))
                    nc.scalar.activation(junk[:, :], xs[:, t, :], ACT.Square, bias=st[:, k, 1:2],
                                         accum_out=st[:, k, 2:3]).then_inc(ln_sq.sem, 1)

            def silu_of(l, par, used):
                act.wait_ge(split_free.sem, split_free.at(l, used))
                nc.scalar.activation(silu[:, par, :], bank[par][:, 0:DE], ACT.Silu).then_inc(silu_ready.sem, 1)

            def cur_of(l, g, h):
                src = xg[:, 4 * h:4 * h + 4, g, :] if isinstance(g, int) else \
                    xg[:, 4 * h:4 * h + 4, bass.ds(g, 1), :].rearrange("p k a s -> p k (a s)")
                nc.scalar.activation(cur_hi[:, 4 * h:4 * h + 4, :], src, ACT.Copy).then_inc(cur_a.sem, 1)

            def aT_of(l, e, par):
                act.wait_ge(at_done.sem, at_done.at(l, e + 1))
                nc.scalar.activation(aT_hi[:, par, :, :], bank[2 + par][:, 0:2 * P].rearrange("p (c t) -> p c t", c=2),
                                     ACT.Copy).then_inc(aT_a.sem, 1)

            def y_of(l, g, used):
                act.wait_ge(split_free.sem, split_free.at(l, used))
                for h in range(2):
                    dst = y_hi[:, g, :] if isinstance(g, int) else y_hi[:, bass.ds(g, 1), :].rearrange("p a n -> p (a n)")
                    nc.scalar.activation(dst[:, 512 * h:512 * h + 512], bank[4 + h][:, :], ACT.Copy).then_inc(y_a.sem, 1)

            def expert_turn(l, e, par, first, p=None, base=0, y=None):
                split_hi(act, l, first, p)
                split_hi(act, l, first + 1, p)
                silu_of(l, par, base - 2)
                split_hi(act, l, first + 2, p)
                split_hi(act, l, first + 3, p)
                aT_of(l, e, par)
                if y is not None:
                    y_of(l, y, base)
                split_hi(act, l, first + 4, p)
                split_hi(act, l, first + 5, p)

            with act.Fori(0, L) as l:
                split_hi(act, l, 0)
                split_hi(act, l, 1)
                turn_x(l, "XT0", 0)
                turn_x(l, "XT1", 1)
                split_hi(act, l, 2)
                split_hi(act, l, 3)
                for i in range(4, 8):
                    split_hi(act, l, i)
                wait_job(l, "A")
                for t, b in enumerate(banks("A")):
                    for g, (c0, n) in enumerate(((0, QR), (QR, KVR))):
                        nc.scalar.activation(junk[:, t * 512 + c0:t * 512 + c0 + n], b[:, c0:c0 + n], ACT.Square,
                                             scale=float(n) ** -0.5, accum_out=sm1[:, g, t:t + 1]).then_inc(job_a.sem, 1)
                    nc.scalar.activation(kf[:, t, :], b[:, QR + KVR:A_ALL], ACT.Copy).then_inc(job_a.sem, 1)
                for i in range(8, 10):
                    split_hi(act, l, i)
                act.wait_ge(fz_v.sem, fz_v.at(l, 2))
                nc.scalar.activation(fz[:, 2, :], fz[:, 1, :], ACT.Exp, scale=-1.0).then_inc(fz_a.sem, 1)
                act.wait_ge(fz_a.sem, fz_a.at(l, 1))
                nc.scalar.activation(fz[:, 3, :], fz[:, 2, :], ACT.Ln, bias=1.0).then_inc(fz_a.sem, 1)
                for i in range(10, 12):
                    split_hi(act, l, i)
                copy_job(l, "FQ", lambda t: fq[:, t, :, 0:HD], lambda b: heads_of(b, FOX_H, HD))
                for i in range(12, 14):
                    split_hi(act, l, i)
                wait_job(l, "LT")
                for t, b in enumerate(banks("LT")):
                    nc.scalar.activation(latT_hi[:, :, t * P:(t + 1) * P],
                                         b[:, 0:3 * P].rearrange("p (k m) -> p k m", k=3), ACT.Copy).then_inc(job_a.sem, 1)
                for i in range(14, 16):
                    split_hi(act, l, i)
                    if i == 14:
                        copy_job(l, "UQ", lambda t: mq[:, t, :, :], lambda b: heads_of(b, MLA_H, MLA_D))
                nc.scalar.activation(st[:, 7, 1:2], mhalf[:, 0:1], ACT.Exp).then_inc(warmed, 1)
                for s in range(HEADS + 3):
                    for i in ahead_of[s]:
                        split_hi(act, l, i)
                    if index["FV", 3] in turns[s]:
                        copy_job(l, "FV", lambda t: fv[:, t, :, :], lambda b: heads_of(b, FOX_H, HD))
                    if index["DQ", 3] in turns[s]:
                        copy_job(l, "DQ", lambda t: dq[:, t, :, :], lambda b: heads_of(b, DIL_H, HD))
                    if index["DK", 3] in turns[s]:
                        copy_job(l, "DK", lambda t: dk[:, t, :, :], lambda b: heads_of(b, DIL_H, HD))
                    for nm, r in (("MK0", 0), ("MK1", 1)):
                        if index[nm, 3] in turns[s]:
                            wait_job(l, nm)
                            for u, b in enumerate(banks(nm)):
                                nc.scalar.activation(kTx[:, 4 * r + 2 * u:4 * r + 2 * u + 2, :],
                                                     b[:, :].rearrange("p (c t) -> p c t", c=2), ACT.Copy)\
                                    .then_inc(job_a.sem, 1)
                    if s < HEADS:
                        evac_qk(l, s)
                    if 1 <= s <= HEADS:
                        exps(l, s - 1)
                    if s >= 3 and (s - 3) % 2 == 1:
                        evac_o(l, s - 3)
                for i in range(index["WO0", 2], index["XQ0", 0]):
                    split_hi(act, l, i)
                square(l, 0)
                for i in range(index["XQ0", 0], index["XQ1", 0]):
                    split_hi(act, l, i)
                turn_x(l, "XT0b", 0)
                turn_x(l, "XT1b", 1)
                for i in range(index["XQ1", 0], index["XQ1", 3] + 1):
                    split_hi(act, l, i)
                    if i == index["XQ1", 1]:
                        wait_job(l, "XQ0")
                        for u, b in enumerate(banks("XQ0")):
                            nc.scalar.activation(qTx[:, 2 * u:2 * u + 2, :], b[:, :].rearrange("p (c t) -> p c t", c=2),
                                                 ACT.Copy).then_inc(job_a.sem, 1)
                for s in range(X_H + 2):
                    if s < X_H:
                        exps(l, HEADS + s)
                    if s == 1:
                        wait_job(l, "XQ1")
                        for u, b in enumerate(banks("XQ1")):
                            nc.scalar.activation(qTx[:, 4 + 2 * u:6 + 2 * u, :],
                                                 b[:, :].rearrange("p (c t) -> p c t", c=2), ACT.Copy)\
                                .then_inc(job_a.sem, 1)
                    if 1 <= s <= 4:
                        split_hi(act, l, index["XO0", s - 1])
                    if s >= 2:
                        evac_o(l, HEADS + s - 2)
                for i in range(index["XO1", 0], N1):
                    split_hi(act, l, i)
                for i in range(N1, N1 + 2):
                    split_hi(act, l, i)
                square(l, 1)
                turn_x(l, "XT0c", 0)
                turn_x(l, "XT1c", 1)
                wait_job(l, "RT")
                nc.scalar.activation(logitT[0:NE, :], bank[2 * pair["RT"]][0:NE, 0:T], ACT.Copy).then_inc(job_a.sem, 1)
                wait_job(l, "GT")
                nc.scalar.activation(rt[:, 0, :], bank[2 * pair["GT"]][:, 0:TT * NE], ACT.Exp, scale=-1.0)\
                    .then_inc(job_a.sem, 1)
                for t in range(TT):
                    nc.scalar.activation(xs_hi[:, t, :], xs[:, t, :], ACT.Copy).then_inc(xs_a.sem, 1)
                nc.scalar.activation(st[:, 7, 0:1], mhalf[:, 0:1], ACT.Silu).then_inc(warmed, 1)
                for i in range(N1 + 2, N1 + 4):
                    split_hi(act, l, i)
                for f in range(0, KC, 2):
                    act.wait_ge(xg_done.sem, xg_done.at(l, f + 1))
                    nc.scalar.activation(xg[:, f, :, :].rearrange("p g s -> p (g s)"), bank[XG_BANK[f]][:, :], ACT.Copy)\
                        .then_inc(xg_a.sem, 1)
                    if f % 4 == 2:
                        act.wait_ge(xg_a.sem, xg_a.at(l, f // 2 + 1))
                        act.wait_ge(xg_v.sem, xg_v.at(l, f // 2 + 1))
                        cur_of(l, 0, f // 4)
                for i in range(N1 + 4, N1 + 6):
                    split_hi(act, l, i)
                act.wait_ge(selT_done.sem, selT_done.at(l, 1))
                for k in range(2):
                    nc.scalar.activation(selT[:, 2 * k:2 * k + 2, :], bank[6 + k][:, :].rearrange("p (g t) -> p g t", g=2),
                                         ACT.Copy).then_inc(selT_a.sem, 1)
                silu_of(l, 0, N1 + 4)
                for i in range(N1 + 6, N1 + 8):
                    split_hi(act, l, i)
                aT_of(l, 0, 0)
                for i in range(N1 + 8, N1 + 10):
                    split_hi(act, l, i)
                with act.Fori(0, TURNS) as p:
                    for j in range(EPG):
                        expert_turn(l, p * EPG + (j + 1), (j + 1) % 2, 6 * j, p, p * N_BODY + (N1 + N_PRO + 6 * j),
                                    p if j == EPG - 1 else None)
                        if j == 1:
                            act.wait_ge(split_free.sem, split_free.at(l, p * N_BODY + (N1 + N_PRO + 6 * j + 4)))
                            for h in range(2):
                                cur_of(l, p + 1, h)
                for j in range(2):
                    expert_turn(l, NE - 3 + j, (NE - 3 + j) % 2, NSUB - N_EPI + 6 * j, None, NSUB - N_EPI + 6 * j)
                split_hi(act, l, NSUB - 2)
                split_hi(act, l, NSUB - 1)
                silu_of(l, 1, NSUB - 4)
                aT_of(l, NE - 1, 1)
                y_of(l, NG - 1, NSUB)
                over = overflow(act, l, paused_a)
                with act.If(over > 0):
                    with act.Fori(0, EPG) as e:
                        act.wait_ge(ov_upped.sem, ov_upped.at(l, e + 1))
                        nc.scalar.activation(silu[:, 0, :], bank[6][:, 0:DE], ACT.Silu).then_inc(ov_silu.sem, 1)
                with act.If(over < 1):
                    act.nop().then_inc(ov_silu.sem, ov_silu.per)
                square(l, 2)

        @block.vector
        def _(dve):
            n = [0]

            def then(ins):
                ins.then_inc(const_v, 1)
                n[0] += 1
                dve.wait_ge(const_v, n[0])

            dve.nop().then_inc(lo_ready.sem, RAW)
            dve.wait_ge(pos_in, 16)
            dve.wait_ge(const_pool, 32)
            TWO_PI = 2 * np.pi
            C1 = 6.28125
            C2 = float(np.float32(np.round((TWO_PI - C1) * 2 ** 17) / 2 ** 17))
            C3 = float(TWO_PI - C1 - C2)
            MAGIC = 1.5 * 2.0 ** 23
            PI_LO = float(np.nextafter(np.float32(np.pi), np.float32(0)))
            a = [ang[:, i, :] for i in range(8)]
            then(nc.vector.tensor_copy(st[:, 6, 0:TT], pos_i[:, :]))
            for t in range(TT):
                then(nc.vector.tensor_scalar(ang[:, 0, t * 32:(t + 1) * 32], freq[:, t, :], st[:, 6, t:t + 1], None, ALU.mult))
            then(nc.vector.tensor_scalar(a[1], a[0], 1.0 / TWO_PI, MAGIC, ALU.mult, ALU.add))
            then(nc.vector.tensor_scalar(a[1], a[1], MAGIC, None, ALU.subtract))
            for cc in (C1, C2, C3):
                then(nc.vector.scalar_tensor_tensor(a[0], a[1], -cc, a[0], ALU.mult, ALU.add))
            then(nc.vector.tensor_scalar(a[6], a[0], PI_LO, -PI_LO, ALU.min, ALU.max))
            then(nc.vector.tensor_scalar(a[2], a[0], float(np.pi / 2), None, ALU.add))
            then(nc.vector.tensor_scalar(a[3], a[2], float(np.pi), -TWO_PI, ALU.is_gt, ALU.mult))
            then(nc.vector.tensor_tensor(a[2], a[2], a[3], ALU.add))
            then(nc.vector.tensor_scalar(a[7], a[2], PI_LO, -PI_LO, ALU.min, ALU.max))
            dve.nop().then_inc(angles, 1)
            dve.wait_ge(bias_in, 16)
            dve.wait_ge(const_pool, 45)
            for k, (_, d) in enumerate(DIL[1:]):
                nc.vector.tensor_scalar(offs2[:, k, :], offs[:, :], d - 1, None, ALU.bitwise_and).then_inc(strides, 1)
            for k in range(4):
                dve.wait_ge(mem_a, k + 1)
                t, h = k // 2, k % 2
                nc.vector.tensor_tensor(memT_lo[:, 4 * h:4 * h + 4, t * P:(t + 1) * P],
                                        bank[4 + k][:, :].rearrange("p (k m) -> p k m", k=4),
                                        memT_hi[:, 4 * h:4 * h + 4, t * P:(t + 1) * P].bitcast(F32), ALU.subtract)\
                    .then_inc(mem_v, 1)
            dve.nop().then_inc(tables, 1)

            def wait_job(l, name):
                dve.wait_ge(*job_done(l, name))

            def turn_x(l, name, t):
                for h, b in enumerate(banks(name)):
                    dve.wait_ge(job_a.sem, job_a.at(l, evac_a[job[name]] - 1 + h))
                    hi = xT_hi[:, 4 * h:4 * h + 4, t * P:(t + 1) * P]
                    nc.vector.tensor_tensor(xT_lo[:, 4 * h:4 * h + 4, t * P:(t + 1) * P],
                                            b[:, :].rearrange("p (k m) -> p k m", k=4), hi.bitcast(F32), ALU.subtract)\
                        .then_inc(job_v.sem, 1)

            def copy_job(l, name, dst, w):
                wait_job(l, name)
                for t, b in enumerate(banks(name)):
                    nc.vector.tensor_copy(dst(t), w(b)).then_inc(job_v.sem, 1)

            def heads_of(b, n_, d):
                return b[:, 0:n_ * d].rearrange("p (h d) -> p h d", h=n_)

            def softmax_max(l, h):
                dve.wait_ge(s_done.sem, s_done.at(l, h + 1))
                if h < HEADS:
                    if h >= 2:
                        dve.wait_ge(pt_done.sem, pt_done.at(l, h - 1))
                    dve.nop().then_inc(paused_v, 1)
                    mask = dilmask if h >= MLA_H + FOX_H else causal
                    scale = float(MLA_D if h < MLA_H else HD) ** -0.5
                    for t in range(TT):
                        sl = slice(0, P) if t == 0 else slice(P, 3 * P)
                        nc.vector.tensor_tensor_reduce(p_sb[:, h % 2, sl], B_S[:, sl], mask[:, P - P * t:2 * P], scale, -3e38,
                                                       ALU.add, ALU.max, mx[:, h, t:t + 1]).then_inc(s_masked.sem, 1)
                    dve.wait_ge(s_masked.sem, s_masked.at(l, 2 * h + 2))
                    nc.vector.tensor_scalar(nmx[:, h, :], mx[:, h, :], -1.0, None, ALU.mult).then_inc(nmx_ready.sem, 1)
                else:
                    nc.vector.tensor_reduce(mx[:, h, :], score_bank(h)[:, :].rearrange("p (t n) -> p t n", t=TT), AX, ALU.max)\
                        .then_inc(s_masked.sem, 1)
                    dve.wait_ge(s_masked.sem, s_masked.at(l, HEADS + h + 1))
                    nc.vector.tensor_scalar(nmx[:, h, :], mx[:, h, :], -1.0 / 16.0, None, ALU.mult)\
                        .then_inc(nmx_ready.sem, 1)

            def softmax_norm(l, h):
                dve.wait_ge(e_ready.sem, e_ready.at(l, 2 * h + 2))
                if MLA_H + FOX_H <= h < HEADS:
                    dve.nop().then_inc(paused_v, 1)
                    k = h - MLA_H - FOX_H
                    for t in range(TT):
                        sl = slice(0, P) if t == 0 else slice(P, 3 * P)
                        nc.vector.tensor_tensor_reduce(p_sb[:, h % 2, sl], p_sb[:, h % 2, sl], dilcount[:, P - P * t:2 * P], 1.0, 0.0,
                                                       ALU.mult, ALU.add, sm[:, h, t:t + 1]).then_inc(counted.sem, 1)
                    dve.wait_ge(counted.sem, counted.at(l, 2 * k + 2))
                nc.vector.reciprocal(ri[:, h, :], sm[:, h, :]).then_inc(ri_ready.sem, 1)
                dve.wait_ge(ri_ready.sem, ri_ready.at(l, h + 1))
                for t in range(TT):
                    sl = (slice(0, P) if t == 0 else slice(P, 3 * P)) if h < HEADS else slice(t * T, (t + 1) * T)
                    nc.vector.tensor_scalar(p_sb[:, h % 2, sl], p_sb[:, h % 2, sl], ri[:, h, t:t + 1], None, ALU.mult)\
                        .then_inc(p_ready.sem, 1)

            def evac_pT(l, h):
                dve.wait_ge(pt_done.sem, pt_done.at(l, h + 1))
                if h >= 2:
                    dve.wait_ge(o_done.sem, o_done.at(l, h - 1))
                w = 3 * P if h < HEADS else 4 * P
                nc.vector.tensor_copy(pT[:, h % 2, 0:w], B_PT[:, 0:w]).then_inc(pT_ready.sem, 1)

            def evac_o(l, h):
                n_ = h // 2 if h < HEADS else h - HEADS // 2
                dve.wait_ge(o_hi.sem, o_hi.at(l, n_ + 1))
                if h < HEADS:
                    o, b = slice(h // 2, h // 2 + 1), B_O[:, 0:T].unsqueeze(1)
                else:
                    k = 2 * (h - HEADS)
                    o, b = slice(k, k + 2), B_O[:, :].rearrange("p (c t) -> p c t", c=2)
                nc.vector.tensor_tensor(mixT_lo[:, o, :], b, mixT_hi[:, o, :].bitcast(F32), ALU.subtract)\
                    .then_inc(o_lo.sem, 1)

            def add(l, n_, t, h, product, signal_):
                half = xs[:, t, 512 * h:512 * h + 512]
                nc.vector.scalar_tensor_tensor(half, half, ALPHA, product, ALU.mult, ALU.add,
                                               accum_out=st[:, 2 * n_ + t, 2 * h:2 * h + 1]).then_inc(signal_.sem, 1)

            def mean(l, n_, t):
                k = 2 * n_ + t
                nc.vector.tensor_scalar(st[:, k, 1:2], st[:, k, 0:1], st[:, k, 2:3], -1.0 / DM, ALU.add, ALU.mult)\
                    .then_inc(ln_nmean.sem, 1)

            def add_first(l, n_, name):
                wait_job(l, name)
                for t, b in enumerate(banks(name)):
                    add(l, n_, t, 0, b[:, :], job_v)

            def add_second(l, n_, name):
                wait_job(l, name)
                for t, b in enumerate(banks(name)):
                    add(l, n_, t, 1, b[:, :], job_v)
                    dve.wait_ge(job_v.sem, job_v.at(l, evac_v[job[name]] - 1 + t))
                    mean(l, n_, t)

            def add_experts(l):
                dve.wait_ge(summed.sem, summed.at(l, 2))
                for t in range(TT):
                    for h in range(2):
                        add(l, 2, t, h, bank[2 * t + h][:, :], acc_read)
                    dve.wait_ge(acc_read.sem, acc_read.at(l, 2 * t + 2))
                    mean(l, 2, t)

            def scale(l, n_, t):
                k = 2 * n_ + t
                dve.wait_ge(gb_in.sem, gb_in.at(l, 32 * (n_ + 1)))
                dve.wait_ge(ln_nmean.sem, ln_nmean.at(l, k + 1))
                nc.vector.scalar_tensor_tensor(scaled[:, t, :], xs[:, t, :], st[:, k, 1:2], gb[:, 0, :],
                                               ALU.add, ALU.mult).then_inc(ln_scaled.sem, 1)

            def norm_x(l, n_, t):
                k = 2 * n_ + t
                dve.wait_ge(ln_scaled.sem, ln_scaled.at(l, k + 1))
                dve.wait_ge(ln_rstd.sem, ln_rstd.at(l, 2 * k + 2))
                nc.vector.scalar_tensor_tensor(xs[:, t, :], scaled[:, t, :], st[:, k, 3:4], gb[:, 1, :],
                                               ALU.mult, ALU.add).then_inc(x_ready.sem, 1)

            def rest_of_norm(l, n_):
                norm_x(l, n_, 0)
                scale(l, n_, 1)
                norm_x(l, n_, 1)

            R = [rt[:, i, :] for i in range(24)]
            q = [0]
            g = R[3].rearrange("p (g i) -> p g i", i=EPG)

            def G4(v):
                return v[:, 0:TT * NG]

            def first_best(step, v, n_, dst, cand, scratch, desc):
                v3 = v.rearrange("p (t n) -> p t n", t=TT)
                step(nc.vector.tensor_reduce(scratch, v3, AX, ALU.max))
                for t in range(TT):
                    step(nc.vector.tensor_scalar(cand[:, t * n_:(t + 1) * n_], v[:, t * n_:(t + 1) * n_],
                                                 scratch[:, t:t + 1], None, ALU.is_equal))
                step(nc.vector.tensor_tensor(cand, cand, desc, ALU.mult))
                step(nc.vector.tensor_reduce(scratch, cand.rearrange("p (t n) -> p t n", t=TT), AX, ALU.max))
                for t in range(TT):
                    step(nc.vector.tensor_scalar(dst[:, t * n_:(t + 1) * n_], cand[:, t * n_:(t + 1) * n_],
                                                 scratch[:, t:t + 1], None, ALU.is_equal))

            def router_groups(l):
                q[0] = 0

                def step(ins):
                    ins.then_inc(route.sem, 1)
                    q[0] += 1
                    dve.wait_ge(route.sem, route.at(l, q[0]))

                dve.wait_ge(job_a.sem, job_a.at(l, evac_a[job["GT"]]))
                step(nc.vector.tensor_scalar(R[1], R[0], 1.0, None, ALU.add))
                step(nc.vector.reciprocal(R[2], R[1]))
                for t in range(TT):
                    step(nc.vector.tensor_tensor(R[3][:, t * NE:(t + 1) * NE], R[2][:, t * NE:(t + 1) * NE],
                                                 rbias[:, :], ALU.add))
                e0, e1_, e2_, e3_ = (g[:, :, i] for i in range(4))
                M, m, N, n2 = (G4(R[i]) for i in range(4, 8))
                nc.vector.tensor_tensor(M, e0, e1_, ALU.max)
                nc.vector.tensor_tensor(m, e0, e1_, ALU.min)
                nc.vector.tensor_tensor(N, e2_, e3_, ALU.max)
                step(nc.vector.tensor_tensor(n2, e2_, e3_, ALU.min))
                top, s1, s2 = (G4(R[i]) for i in range(8, 11))
                nc.vector.tensor_tensor(top, M, N, ALU.max)
                nc.vector.tensor_tensor(s1, M, N, ALU.min)
                step(nc.vector.tensor_tensor(s2, m, n2, ALU.max))
                step(nc.vector.tensor_tensor(s1, s1, s2, ALU.max))
                step(nc.vector.tensor_tensor(s2, top, s1, ALU.add))

                first_best(step, s2, NG, ing[:, :], G4(R[12]), R[13][:, 0:TT], desc4[:, :])
                assert q[0] == group_at, q[0]
                dve.wait_ge(ranked.sem, ranked.at(l, 1))
                pg = posg[:, :, :].rearrange("p t g -> p (t g)")
                step(nc.vector.tensor_tensor(pg, bank[4][:, 0:TT * NG], ing[:, :], ALU.mult))
                step(nc.vector.tensor_scalar(pg, pg, -1.0, None, ALU.add))
                for t in range(TT):
                    nc.vector.tensor_tensor(sel[:, t, :].rearrange("p (g s) -> p g s", g=NG),
                                            iota[:, :].unsqueeze(1).to_broadcast([P, NG, P]),
                                            posg[:, t, :].unsqueeze(2).to_broadcast([P, NG, P]), ALU.is_equal)\
                        .then_inc(sel_ready.sem, 1)
                return step

            def router_first(l, step):
                b3 = ing[:, :].unsqueeze(2).to_broadcast([P, TT * NG, EPG])
                step(nc.vector.tensor_scalar(G4(R[14]), ing[:, :], -1.0, BIG, ALU.add, ALU.mult))
                o3 = G4(R[14]).unsqueeze(2).to_broadcast([P, TT * NG, EPG])
                k3 = R[15].rearrange("p (g i) -> p g i", i=EPG)
                step(nc.vector.tensor_tensor(k3, g, b3, ALU.mult))
                step(nc.vector.tensor_tensor(k3, k3, o3, ALU.add))
                first_best(step, R[15], NE, R[16], R[17], R[13][:, 0:TT], desc16[:, :])

            def router_gates(l, step):
                step(nc.vector.scalar_tensor_tensor(R[18], R[16], -2.0 * BIG, R[15], ALU.mult, ALU.add))
                first_best(step, R[18], NE, R[19], R[17], R[13][:, 0:TT], desc16[:, :])
                step(nc.vector.tensor_tensor(R[20], R[16], R[19], ALU.add))
                step(nc.vector.tensor_tensor(R[21], R[20], R[2], ALU.mult))
                step(nc.vector.tensor_reduce(R[13][:, 0:TT], R[21].rearrange("p (t n) -> p t n", t=TT), AX, ALU.add))
                step(nc.vector.reciprocal(R[13][:, 2:2 + TT], R[13][:, 0:TT]))
                for t in range(TT):
                    step(nc.vector.tensor_scalar(gates[:, t, :], R[21][:, t * NE:(t + 1) * NE],
                                                 R[13][:, 2 + t:3 + t], None, ALU.mult))
                gg = gates[:, :, :].rearrange("p t (g i) -> p t g i", i=EPG)
                for g_ in range(1, NG):
                    a0 = gg[:, :, 0, :] if g_ == 1 else g4[:, :, :]
                    step(nc.vector.tensor_tensor(g4[:, :, :], a0, gg[:, :, g_, :], ALU.add))
                step(nc.vector.tensor_scalar(fl[:, 0:NG], bank[4][:, TT * NG:TT * NG + NG], P + 0.5, None, ALU.is_gt))
                step(nc.vector.tensor_tensor(fl[:, NG:2 * NG], fl[:, 0:NG], iota[:, 0:NG], ALU.mult))
                step(nc.vector.tensor_reduce(fl[:, 2 * NG:2 * NG + 2], fl[:, 0:2 * NG].rearrange("p (a g) -> p a g", a=2),
                                             AX, ALU.add))
                assert q[0] == route.per, q[0]
                nc.vector.tensor_copy(flag[0:1, 0:2], fl[0:1, 2 * NG:2 * NG + 2]).then_inc(flag_ready.sem, 3)

            def act_of(l, e, par):
                dve.wait_ge(silu_ready.sem, silu_ready.at(l, e + 1))
                nc.vector.scalar_tensor_tensor(act_a[:, par, :], silu[:, par, :], gs[:, bass.ds(e, 1)],
                                               bank[par][:, DE:2 * DE], ALU.mult, ALU.mult).then_inc(a_ready.sem, 1)

            def cur_of(l, g, h):
                dve.wait_ge(cur_a.sem, cur_a.at(l, g * 2 + (h + 1)))
                src = xg[:, 4 * h:4 * h + 4, g, :] if isinstance(g, int) else \
                    xg[:, 4 * h:4 * h + 4, bass.ds(g, 1), :].rearrange("p k a s -> p k (a s)")
                nc.vector.tensor_tensor(cur_lo[:, 4 * h:4 * h + 4, :], src, cur_hi[:, 4 * h:4 * h + 4, :].bitcast(F32),
                                        ALU.subtract).then_inc(cur_v.sem, 1)

            def aT_of(l, e, par):
                dve.wait_ge(aT_a.sem, aT_a.at(l, e + 1))
                nc.vector.tensor_tensor(aT_lo[:, par, :, :], bank[2 + par][:, 0:2 * P].rearrange("p (c t) -> p c t", c=2),
                                        aT_hi[:, par, :, :].bitcast(F32), ALU.subtract).then_inc(aT_v.sem, 1)

            def y_of(l, g):
                for h in range(2):
                    dve.wait_ge(y_a.sem, y_a.at(l, g * 2 + (h + 1)))
                    hi, lo = (v[:, g, :] if isinstance(g, int) else v[:, bass.ds(g, 1), :].rearrange("p a n -> p (a n)")
                              for v in (y_hi, y_lo))
                    c = slice(512 * h, 512 * h + 512)
                    nc.vector.tensor_tensor(lo[:, c], bank[4 + h][:, :], hi[:, c].bitcast(F32), ALU.subtract)\
                        .then_inc(y_v.sem, 1)

            def further_tokens(l):
                nc.vector.tensor_reduce(pos1[:, :], posg[:, :, :], AX, ALU.max).then_inc(ov_picked.sem, 1)
                dve.wait_ge(ov_picked.sem, ov_picked.at(l, 1))
                for t in range(TT):
                    nc.vector.tensor_scalar(ov_sel[:, t, :], iota[:, :], float(P), pos1[:, t:t + 1], ALU.add, ALU.is_equal)\
                        .then_inc(ov_picked.sem, 1)
                dve.wait_ge(ov_gathered.sem, ov_gathered.at(l, 1))
                for h in range(2):
                    nc.vector.tensor_copy(ov_x[:, 4 * h:4 * h + 4, :], bank[4 + h][:, :].rearrange("p (k s) -> p k s", k=4))\
                        .then_inc(ov_kept.sem, 1)
                nc.vector.tensor_copy(ov_selT[:, :], bank[6][:, 0:T]).then_inc(ov_kept.sem, 1)
                nc.vector.tensor_copy(ov_gs[:, :], bank[7][:, 0:EPG]).then_inc(ov_kept.sem, 2)
                nc.vector.memset(ov_y[:, :], 0.0).then_inc(ov_y_in.sem, 1)
                dve.wait_ge(ov_kept.sem, ov_kept.at(l, 5))
                dve.nop().then_inc(paused_v, 1)
                with dve.Fori(0, EPG) as e:
                    dve.wait_ge(ov_silu.sem, ov_silu.at(l, e + 1))
                    nc.vector.scalar_tensor_tensor(act_a[:, 0, :], silu[:, 0, :], ov_gs[:, bass.ds(e, 1)],
                                                   bank[6][:, DE:2 * DE], ALU.mult, ALU.mult).then_inc(ov_act.sem, 1)
                    dve.wait_ge(ov_turned.sem, ov_turned.at(l, e + 1))
                    nc.vector.tensor_copy(ov_aT[:, :, :], bank[7][:, 0:2 * P].rearrange("p (c s) -> p c s", c=2))\
                        .then_inc(ov_aT_in.sem, 1)
                    dve.wait_ge(ov_used.sem, ov_used.at(l, e + 1))
                    dve.wait_ge(ov_y_in.sem, ov_y_in.at(l, e * 2 + 1))
                    for h in range(2):
                        c = slice(512 * h, 512 * h + 512)
                        nc.vector.tensor_tensor(ov_y[:, c], ov_y[:, c], bank[4 + h][:, :], ALU.add).then_inc(ov_y_in.sem, 1)

            def expert_turn(l, e, par, first, p=None, y=None):
                split_lo(dve, l, first, p)
                split_lo(dve, l, first + 1, p)
                act_of(l, e, par)
                split_lo(dve, l, first + 2, p)
                split_lo(dve, l, first + 3, p)
                aT_of(l, e, par)
                if y is not None:
                    y_of(l, y)
                split_lo(dve, l, first + 4, p)
                split_lo(dve, l, first + 5, p)

            with dve.Fori(0, L) as l:
                split_lo(dve, l, 0)
                split_lo(dve, l, 1)
                turn_x(l, "XT0", 0)
                turn_x(l, "XT1", 1)
                split_lo(dve, l, 2)
                split_lo(dve, l, 3)
                for i in range(4, 8):
                    split_lo(dve, l, i)
                dve.wait_ge(small_in.sem, small_in.at(l, 48))
                dve.wait_ge(rms_step.sem, rms_step.at(l, 2))
                for t, b in enumerate(banks("A")):
                    for g_, (c0, w) in enumerate(((0, QR), (QR, KVR))):
                        nc.vector.scalar_tensor_tensor(lat[:, t, c0:c0 + w], b[:, c0:c0 + w], sm1[:, 2 + g_, t:t + 1],
                                                       gains[:, c0:c0 + w], ALU.mult, ALU.mult).then_inc(job_v.sem, 1)
                z3 = lambda i: fz[:, i, :].rearrange("p (t f) -> p t f", t=TT)
                nc.vector.tensor_tensor(z3(0), kf[:, :, ROPE:], bforget[:, :].unsqueeze(1).to_broadcast([P, TT, FOX_H]),
                                        ALU.add).then_inc(fz_v.sem, 1)
                dve.wait_ge(fz_v.sem, fz_v.at(l, 1))
                nc.vector.scalar_tensor_tensor(fz[:, 1, :], fz[:, 0, :], -1.0, fz[:, 0, :], ALU.mult, ALU.max).then_inc(fz_v.sem, 1)
                for i in range(8, 10):
                    split_lo(dve, l, i)
                dve.wait_ge(fz_a.sem, fz_a.at(l, 2))
                nc.vector.scalar_tensor_tensor(fz[:, 1, :], fz[:, 0, :], 0.0, fz[:, 3, :], ALU.min, ALU.subtract)\
                    .then_inc(fz_v.sem, 1)
                for i in range(10, 14):
                    split_lo(dve, l, i)
                copy_job(l, "FK", lambda t: fk[:, t, :, 0:HD], lambda b: heads_of(b, FOX_H, HD))
                for t, b in enumerate(banks("LT")):
                    dve.wait_ge(job_a.sem, job_a.at(l, evac_a[job["LT"]] - 1 + t))
                    nc.vector.tensor_tensor(latT_lo[:, :, t * P:(t + 1) * P],
                                            b[:, 0:3 * P].rearrange("p (k m) -> p k m", k=3),
                                            latT_hi[:, :, t * P:(t + 1) * P].bitcast(F32), ALU.subtract)\
                        .then_inc(job_v.sem, 1)
                    f = b[:, 3 * P:3 * P + FOX_H].unsqueeze(2)
                    nc.vector.tensor_scalar(fq[:, t, :, HD:HD + 1], f, float(HD) ** 0.5, None, ALU.mult)\
                        .then_inc(job_v.sem, 1)
                    nc.vector.tensor_scalar(fk[:, t, :, HD + 1:HD + 2], f, -float(HD) ** 0.5, None, ALU.mult)\
                        .then_inc(job_v.sem, 1)
                for i in range(14, 16):
                    split_lo(dve, l, i)
                    if i == 15:
                        wait_job(l, "UKV")
                        for t, b in enumerate(banks("UKV")):
                            kv = b[:, :].rearrange("p (h d) -> p h d", h=MLA_H)
                            nc.vector.tensor_copy(mk[:, t, :, 0:HD], kv[:, :, 0:HD]).then_inc(job_v.sem, 1)
                            nc.vector.tensor_copy(mv[:, t, :, :], kv[:, :, HD:2 * HD]).then_inc(job_v.sem, 1)
                for s in range(HEADS + 3):
                    for i in ahead_of[s]:
                        split_lo(dve, l, i)
                    if index["DV", 3] in turns[s]:
                        copy_job(l, "DV", lambda t: dv[:, t, :, :], lambda b: heads_of(b, DIL_H, HD))
                    if index["MV0", 3] in turns[s]:
                        copy_job(l, "MV0", lambda t: vx[:, t, 0:512], lambda b: b[:, :])
                    if 1 <= s <= HEADS:
                        softmax_max(l, s - 1)
                    if 2 <= s <= HEADS + 1:
                        evac_pT(l, s - 2)
                    if s >= 3 and (s - 3) % 2 == 1:
                        evac_o(l, s - 3)
                    if 1 <= s <= HEADS:
                        softmax_norm(l, s - 1)
                for i in range(index["WO0", 2], index["XQ0", 0]):
                    split_lo(dve, l, i)
                    if i == index["WO1", 1]:
                        add_first(l, 0, "WO0")
                    if i == index["MV1", 1]:
                        add_second(l, 0, "WO1")
                        scale(l, 0, 0)
                        scale(l, 0, 1)
                norm_x(l, 0, 0)
                norm_x(l, 0, 1)
                for i in range(index["XQ0", 0], index["XQ0", 2]):
                    split_lo(dve, l, i)
                copy_job(l, "MV1", lambda t: vx[:, t, 512:1024], lambda b: b[:, :])
                turn_x(l, "XT0b", 0)
                turn_x(l, "XT1b", 1)
                for i in range(index["XQ0", 2], index["XQ1", 3] + 1):
                    split_lo(dve, l, i)
                for s in range(X_H + 2):
                    if s < X_H:
                        softmax_max(l, HEADS + s)
                    if s < X_H:
                        softmax_norm(l, HEADS + s)
                    if 1 <= s <= X_H:
                        evac_pT(l, HEADS + s - 1)
                    if 1 <= s <= 4:
                        split_lo(dve, l, index["XO0", s - 1])
                    if s >= 2:
                        evac_o(l, HEADS + s - 2)
                for i in range(index["XO1", 0], N1):
                    split_lo(dve, l, i)
                    if i == index["XO1", 1]:
                        add_first(l, 1, "XO0")
                add_second(l, 1, "XO1")
                scale(l, 1, 0)
                rest_of_norm(l, 1)
                turn_x(l, "XT0c", 0)
                turn_x(l, "XT1c", 1)
                for i in range(N1, N1 + 2):
                    split_lo(dve, l, i)
                step = router_groups(l)
                for i in range(N1 + 2, N1 + 4):
                    split_lo(dve, l, i)
                router_first(l, step)
                for f in range(1, KC, 2):
                    dve.wait_ge(xg_done.sem, xg_done.at(l, f + 1))
                    nc.vector.tensor_copy(xg[:, f, :, :].rearrange("p g s -> p (g s)"), bank[XG_BANK[f]][:, :])\
                        .then_inc(xg_v.sem, 1)
                    if f % 4 == 3:
                        cur_of(l, 0, f // 4)
                split_lo(dve, l, N1 + 4)
                router_gates(l, step)
                split_lo(dve, l, N1 + 5)
                dve.wait_ge(gs_done.sem, gs_done.at(l, 1))
                nc.vector.tensor_copy(gs[:, :], bank[5][:, 0:NE]).then_inc(gs_ready.sem, 1)
                dve.wait_ge(gs_ready.sem, gs_ready.at(l, 1))
                act_of(l, 0, 0)
                for i in range(N1 + 6, N1 + 8):
                    split_lo(dve, l, i)
                aT_of(l, 0, 0)
                for i in range(N1 + 8, N1 + 10):
                    split_lo(dve, l, i)
                with dve.Fori(0, TURNS) as p:
                    for j in range(EPG):
                        expert_turn(l, p * EPG + (j + 1), (j + 1) % 2, 6 * j, p, p if j == EPG - 1 else None)
                        if j == 1:
                            for h in range(2):
                                cur_of(l, p + 1, h)
                for j in range(2):
                    expert_turn(l, NE - 3 + j, (NE - 3 + j) % 2, NSUB - N_EPI + 6 * j)
                split_lo(dve, l, NSUB - 2)
                split_lo(dve, l, NSUB - 1)
                act_of(l, NE - 1, 1)
                aT_of(l, NE - 1, 1)
                y_of(l, NG - 1)
                over = overflow(dve, l, paused_v)
                with dve.If(over > 0):
                    further_tokens(l)
                with dve.If(over < 1):
                    for s_ in (ov_picked, ov_kept, ov_act, ov_aT_in, ov_y_in):
                        dve.nop().then_inc(s_.sem, s_.per)
                add_experts(l)
                scale(l, 2, 0)
                rest_of_norm(l, 2)

        @block.tensor
        def _(pe):
            pe.wait_ge(const_pool, 45)
            pe.wait_ge(mem_in, 16)
            for n in range(4):
                t, h = n // 2, n % 2
                for k in range(4):
                    f = 4 * h + k
                    ins = nc.tensor.transpose(bank[4 + n][:, k * P:(k + 1) * P], mem_tok[:, t, f * P:(f + 1) * P], ident[:, :])
                ins.then_inc(mem_done, 1)
            pe.wait_ge(start_in, 16)
            pe.nop().then_inc(split_free.sem, SPL)
            pe.nop().then_inc(ov_used.sem, 1)
            pe.nop().then_inc(x_ready.sem, 2)

            def product(o, lhs, rhs, first, last, shared=False):
                nc.tensor.matmul(o, lhs[0], rhs[0], start=first, stop=False, skip_group_check=shared)
                nc.tensor.matmul(o, lhs[0], rhs[1], start=False, stop=False, skip_group_check=shared)
                return nc.tensor.matmul(o, lhs[1], rhs[0], start=False, stop=last, skip_group_check=shared)

            def ready(l, name):
                n = job[name]
                if jobs[n][1]:
                    pe.wait_ge(job_a.sem, job_a.at(l, evac_a[n]))
                if jobs[n][2]:
                    pe.wait_ge(job_v.sem, job_v.at(l, evac_v[n]))

            def open_job(l, name):
                if job[name] >= 2:
                    ready(l, jobs[job[name] - 2][0])

            def sub_in(l, i, p=None):
                pe.wait_ge(lo_ready.sem, lo_ready.at(l, number(i, p) + 1))
                return w_hi[:, split_slot(i, p), :], w_lo[:, split_slot(i, p), :]

            def rows(l, name, j, xhl, w, chunks=None, per=2):
                if j == 0:
                    open_job(l, name)
                parts = sub_in(l, index[name, j])
                chunks = chunks or KC
                for k in range(per):
                    kc = per * j + k
                    r = tuple(v[:, k * w:(k + 1) * w] for v in parts)
                    for t, b in enumerate(banks(name)):
                        lhs = tuple(v[:, kc, t * P:(t + 1) * P] for v in xhl)
                        ins = product(b[:, 0:w], lhs, r, kc == 0, kc == chunks - 1)
                ins.then_inc(split_free.sem, 1)

            def columns(l, name, j, xhl):
                if j == 0:
                    open_job(l, name)
                parts = sub_in(l, index[name, j])
                for k in range(2):
                    kc = 2 * j + k
                    r = tuple(v[:, kc, :] for v in xhl)
                    for cb in range(4):
                        lhs = tuple(v[:, k * 512 + cb * P:k * 512 + (cb + 1) * P] for v in parts)
                        ins = product(banks(name)[cb // 2][:, (cb % 2) * T:(cb % 2 + 1) * T], lhs, r,
                                      kc == 0 and cb % 2 == 0, kc == KC - 1 and cb % 2 == 1, shared=True)
                ins.then_inc(split_free.sem, 1)

            xT, memT, mixT, latT = (xT_hi, xT_lo), (memT_hi, memT_lo), (mixT_hi, mixT_lo), (latT_hi, latT_lo)
            KINDS = {"MK0": (columns, memT), "MK1": (columns, memT), "XQ0": (columns, xT), "XQ1": (columns, xT),
                     "MV0": (rows, memT, 512), "MV1": (rows, memT, 512), "WO0": (rows, mixT, 512),
                     "WO1": (rows, mixT, 512), "XO0": (rows, mixT, 512), "XO1": (rows, mixT, 512),
                     "A": (rows, xT, A_ALL)}

            def gemm(l, i):
                name, j, _ = stream[i]
                if name == "WO0":
                    pe.wait_ge(o_lo.sem, o_lo.at(l, 2 * j + 2))
                if name == "XO0":
                    pe.wait_ge(o_lo.sem, o_lo.at(l, HEADS // 2 + j + 1))
                if name in KINDS:
                    f, *args = KINDS[name]
                    f(l, name, j, *args)
                else:
                    rows(l, name, j, xT, cols[name][1])

            def turn_x(l, name, t, count):
                pe.wait_ge(x_ready.sem, x_ready.at(l, count))
                open_job(l, name)
                for f in range(KC):
                    ins = nc.tensor.transpose(banks(name)[f // 4][:, (f % 4) * P:(f % 4 + 1) * P],
                                              xs[:, t, f * P:(f + 1) * P], ident[:, :])
                ins.then_inc(turned.sem, 1)

            def head_qk(l, h):
                if h == 0:
                    ready(l, "UKV")
                    pe.wait_ge(rope_step.sem, rope_step.at(l, 14))
                if h == MLA_H:
                    ready(l, "FQ")
                    ready(l, "FK")
                    pe.wait_ge(aug.sem, aug.at(l, 2))
                if h == MLA_H + FOX_H:
                    pe.wait_ge(rope_step.sem, rope_step.at(l, 26))
                if h:
                    pe.wait_ge(qkT_ready.sem, qkT_ready.at(l, h))
                q, k, g = ((mq, mk, h) if h < MLA_H else (fq, fk, h - MLA_H) if h < MLA_H + FOX_H else
                           (dq, dk, h - MLA_H - FOX_H))
                d = MLA_D if h < MLA_H else FOX_D if h < MLA_H + FOX_H else DIL_D
                if h >= MLA_H + FOX_H:
                    pe.nop().then_inc(paused_t, 1)
                for n, v in enumerate((q, k)):
                    for t in range(TT):
                        c0 = (2 * n + t) * P
                        ins = nc.tensor.transpose(B_QK[0:d, c0:c0 + P], v[:, t, g, :], ident[:, :])
                ins.then_inc(qk_done.sem, 1)

            def head_scores(l, h):
                if h < HEADS:
                    pe.wait_ge(qkT_ready.sem, qkT_ready.at(l, h + 1))
                    if h:
                        pe.wait_ge(s_masked.sem, s_masked.at(l, 2 * h))
                    d = MLA_D if h < MLA_H else FOX_D if h < MLA_H + FOX_H else DIL_D
                    v = qkT[0:d, h % 2, :]
                    nc.tensor.matmul(B_S[:, 0:P], v[:, 0:P], v[:, 2 * P:3 * P], start=True, stop=True)
                    nc.tensor.matmul(B_S[:, P:3 * P], v[:, P:2 * P], v[:, 2 * P:4 * P], start=True, stop=True)\
                        .then_inc(s_done.sem, 1)
                else:
                    g = h - HEADS
                    if g >= 2:
                        pe.wait_ge(e_ready.sem, e_ready.at(l, 2 * h - 2))
                    o = score_bank(h)
                    for t in range(TT):
                        for c_ in range(2):
                            ins = nc.tensor.matmul(o[:, t * T:(t + 1) * T], qTx[:, 2 * g + c_, t * P:(t + 1) * P],
                                                   kTx[:, 2 * g + c_, :], start=c_ == 0, stop=c_ == 1)
                    ins.then_inc(s_done.sem, 1)

            def head_turn(l, h):
                pe.wait_ge(p_ready.sem, p_ready.at(l, 2 * h + 2))
                if h:
                    pe.wait_ge(pT_ready.sem, pT_ready.at(l, h))
                pr = p_sb[:, h % 2, :]
                if h < HEADS:
                    for k in range(3):
                        ins = nc.tensor.transpose(B_PT[:, k * P:(k + 1) * P], pr[:, k * P:(k + 1) * P], ident[:, :])
                else:
                    for t in range(TT):
                        for c_ in range(2):
                            ins = nc.tensor.transpose(B_PT[:, c_ * T + t * P:c_ * T + (t + 1) * P],
                                                      pr[:, t * T + c_ * P:t * T + (c_ + 1) * P], ident[:, :])
                ins.then_inc(pt_done.sem, 1)

            def head_values(l, h):
                pe.wait_ge(pT_ready.sem, pT_ready.at(l, h + 1))
                if h == MLA_H:
                    ready(l, "FV")
                if h == MLA_H + FOX_H:
                    ready(l, "DV")
                if h < HEADS:
                    if h % 2 == 0 and h:
                        pe.wait_ge(o_lo.sem, o_lo.at(l, h // 2))
                    v, g = ((mv, h) if h < MLA_H else (fv, h - MLA_H) if h < MLA_H + FOX_H else
                            (dv, h - MLA_H - FOX_H))
                    o = B_O[(h % 2) * HD:(h % 2 + 1) * HD, :]
                    nc.tensor.matmul(o[:, 0:T], v[:, 0, g, :], pT[:, h % 2, 0:T], start=True, stop=False)
                    nc.tensor.matmul(o[:, P:T], v[:, 1, g, :], pT[:, h % 2, T:T + P], start=False, stop=True)\
                        .then_inc(o_done.sem, 1)
                else:
                    pe.wait_ge(o_lo.sem, o_lo.at(l, h - HEADS // 2))
                    g = h - HEADS
                    for dblk in range(2):
                        for c_ in range(2):
                            f = 2 * g + dblk
                            ins = nc.tensor.matmul(B_O[:, dblk * T:(dblk + 1) * T], vx[:, c_, f * P:(f + 1) * P],
                                                   pT[:, h % 2, c_ * T:(c_ + 1) * T], start=c_ == 0, stop=c_ == 1)
                    ins.then_inc(o_done.sem, 1)

            def experts_up(l, i, par, js, p=None, g=None):
                for j in js:
                    if g is not None and j % 2 == 0:
                        pe.wait_ge(cur_v.sem, cur_v.at(l, g * 2 + (j // 2 + 1)))
                    parts = sub_in(l, i + j, p)
                    for k in range(2):
                        kc = 2 * j + k
                        lhs = tuple(v[:, kc, :] for v in (cur_hi, cur_lo))
                        r = tuple(v[:, k * 512:(k + 1) * 512] for v in parts)
                        ins = product(bank[par][:, :], lhs, r, kc == 0, kc == KC - 1)
                    ins.then_inc(split_free.sem, 1)

            def turn_a(l, e, par):
                pe.wait_ge(a_ready.sem, a_ready.at(l, e + 1))
                for c_ in range(2):
                    ins = nc.tensor.transpose(bank[2 + par][:, c_ * P:(c_ + 1) * P], act_a[:, par, c_ * P:(c_ + 1) * P],
                                              ident[:, :])
                ins.then_inc(at_done.sem, 1)

            def experts_down(l, e, i, par, first, last, p=None):
                pe.wait_ge(aT_v.sem, aT_v.at(l, e + 1))
                if p is not None and first:
                    pe.wait_ge(y_v.sem, y_v.at(l, p * 2 + 2))
                for c_ in range(2):
                    parts = sub_in(l, i + c_, p)
                    for h in range(2):
                        lhs = (aT_hi[:, par, c_, :], aT_lo[:, par, c_, :])
                        r = tuple(v[:, 512 * h:512 * (h + 1)] for v in parts)
                        ins = product(bank[4 + h][:, :], lhs, r, first and c_ == 0, last and c_ == 1)
                    ins.then_inc(split_free.sem, 1)

            def expert_turn(l, e, j, i, p=None, between=None):
                g = p + 1 if j == EPG - 1 else None
                experts_up(l, i, (j + 1) % 2, (0, 1), p, g)
                if between:
                    between()
                turn_a(l, e, j % 2)
                experts_up(l, i, (j + 1) % 2, (2, 3), p, g)
                experts_down(l, e, i + 4, j % 2, j == 0, j == EPG - 1, p)

            def gather(l):
                pe.wait_ge(route.sem, route.at(l, group_at))
                for t in range(TT):
                    for s in range(t + 1):
                        nc.tensor.matmul(bank[4][:, t * NG:(t + 1) * NG], (ones if s < t else upto)[:, :],
                                         ing[:, s * NG:(s + 1) * NG], start=t == 0, stop=False, skip_group_check=True)
                for s in range(TT):
                    ins = nc.tensor.matmul(bank[4][:, TT * NG:TT * NG + NG], ones[:, :], ing[:, s * NG:(s + 1) * NG],
                                           start=False, stop=s == TT - 1, skip_group_check=True)
                ins.then_inc(ranked.sem, 1)
                pe.wait_ge(xs_p.sem, xs_p.at(l, TT))
                pe.wait_ge(sel_ready.sem, sel_ready.at(l, TT))
                for f in range(KC):
                    if f >= 6:
                        emptied = xg_a if f == 6 else xg_v
                        pe.wait_ge(emptied.sem, emptied.at(l, 2))
                    for n, (v, t) in enumerate((v, t) for v in (xs_hi, xs_lo) for t in range(TT)):
                        ins = nc.tensor.matmul(bank[XG_BANK[f]][:, :], v[:, t, f * P:(f + 1) * P], sel[:, t, :],
                                               start=n == 0, stop=n == 3)
                    ins.then_inc(xg_done.sem, 1)

            def place_gates(l):
                pe.wait_ge(route.sem, route.at(l, route.per))
                for g in range(NG):
                    for t in range(TT):
                        ins = nc.tensor.matmul(bank[5][:, g * EPG:(g + 1) * EPG],
                                               sel[:, t, g * P:(g + 1) * P].bitcast(F32), g4[:, t, :],
                                               start=g == 0 and t == 0, stop=g == NG - 1 and t == 1, skip_group_check=True)
                ins.then_inc(gs_done.sem, 1)

            def turn_sel(l):
                pe.wait_ge(xg_a.sem, xg_a.at(l, KC // 2))
                pe.wait_ge(xg_v.sem, xg_v.at(l, KC // 2))
                for g in range(NG):
                    for t in range(TT):
                        ins = nc.tensor.transpose(bank[6 + g // 2][:, (g % 2) * T + t * P:(g % 2) * T + (t + 1) * P],
                                                  sel[:, t, g * P:(g + 1) * P].bitcast(F32), ident[:, :])
                ins.then_inc(selT_done.sem, 1)

            def scatter(l, g):
                if g == 0:
                    pe.wait_ge(selT_a.sem, selT_a.at(l, 2))
                for h in range(2):
                    pe.wait_ge(y_v.sem, y_v.at(l, 2 * g + h + 1))
                    for t in range(TT):
                        for v in (y_hi, y_lo):
                            ins = nc.tensor.matmul(bank[2 * t + h][:, :], selT[:, g, t * P:(t + 1) * P],
                                                   v[:, g, 512 * h:512 * h + 512], start=g == 0 and v is y_hi,
                                                   stop=g == NG - 1 and v is y_lo, skip_group_check=True)
                if g == NG - 1:
                    ins.then_inc(summed.sem, 1)

            def further_tokens(l):
                pe.wait_ge(ov_picked.sem, ov_picked.at(l, 1 + TT))
                pe.nop().then_inc(paused_t, 1)
                for t in range(TT):
                    nc.tensor.transpose(bank[6][:, t * P:(t + 1) * P], ov_sel[:, t, :], ident[:, :])
                for t in range(TT):
                    nc.tensor.matmul(bank[7][:, 0:EPG], ov_sel[:, t, :], g4[:, t, :], start=t == 0, stop=t == 1)
                for f in range(KC):
                    for t in range(TT):
                        ins = nc.tensor.matmul(bank[4 + f // 4][:, (f % 4) * P:(f % 4 + 1) * P],
                                               xs[:, t, f * P:(f + 1) * P], ov_sel[:, t, :],
                                               start=f % 4 == 0 and t == 0, stop=t == 1, skip_group_check=True)
                ins.then_inc(ov_gathered.sem, 1)
                pe.wait_ge(ov_kept.sem, ov_kept.at(l, 5))
                pe.nop().then_inc(paused_t, 1)
                with pe.Fori(0, EPG) as e:
                    pe.wait_ge(ov_in.sem, e * 48 + ov_in.at(l, 48))
                    for kc in range(KC):
                        ins = nc.tensor.matmul(bank[6][:, :], ov_x[:, kc, :], ov_up[:, kc, :], start=kc == 0, stop=kc == KC - 1)
                    ins.then_inc(ov_upped.sem, 1)
                    pe.wait_ge(ov_act.sem, ov_act.at(l, e + 1))
                    for c_ in range(2):
                        ins = nc.tensor.transpose(bank[7][:, c_ * P:(c_ + 1) * P], act_a[:, 0, c_ * P:(c_ + 1) * P], ident[:, :])
                    ins.then_inc(ov_turned.sem, 1)
                    pe.wait_ge(ov_aT_in.sem, ov_aT_in.at(l, e + 1))
                    for c_ in range(2):
                        for h in range(2):
                            ins = nc.tensor.matmul(bank[4 + h][:, :], ov_aT[:, c_, :], ov_down[:, c_, 512 * h:512 * h + 512],
                                                   start=c_ == 0, stop=c_ == 1)
                    ins.then_inc(ov_used.sem, 1)
                pe.wait_ge(ov_y_in.sem, ov_y_in.at(l, ov_y_in.per))
                pe.nop().then_inc(paused_t, 1)
                for t in range(TT):
                    for h in range(2):
                        ins = nc.tensor.matmul(bank[2 * t + h][:, :], ov_selT[:, t * P:(t + 1) * P],
                                         ov_y[:, 512 * h:512 * h + 512], start=False, stop=True, skip_group_check=True)
                ins.then_inc(summed.sem, 1)

            with pe.Fori(0, L) as l:
                turn_x(l, "XT0", 0, -1)
                turn_x(l, "XT1", 1, 0)
                ready(l, "XT0")
                ready(l, "XT1")
                for i in range(0, 8):
                    gemm(l, i)
                pe.wait_ge(job_v.sem, job_v.at(l, evac_v[job["A"]]))
                pe.wait_ge(fz_v.sem, fz_v.at(l, 3))
                open_job(l, "FK")
                for i in range(8, 12):
                    gemm(l, i)
                open_job(l, "LT")
                for t, b in enumerate(banks("LT")):
                    for k in range(3):
                        nc.tensor.transpose(b[:, k * P:(k + 1) * P], lat[:, t, k * P:(k + 1) * P], ident[:, :])
                    o = b[:, 3 * P:3 * P + FOX_H]
                    lf = fz[:, 1, :].rearrange("p (t f) -> p t f", t=TT)
                    for s in range(t + 1):
                        ins = nc.tensor.matmul(o, (ones if s < t else upto)[:, :], lf[:, s, :], start=s == 0, stop=s == t)
                ins.then_inc(turned.sem, 1)
                open_job(l, "UQ")
                ready(l, "LT")
                rows(l, "UQ", 0, latT, MLA_H * MLA_D, chunks=2)
                rows(l, "UKV", 0, tuple(v[:, 2:3, :] for v in latT), 512, chunks=1, per=1)
                for s in range(HEADS + 3):
                    for i in turns[s]:
                        gemm(l, i)
                    if s >= 3:
                        head_values(l, s - 3)
                    if 2 <= s <= HEADS + 1:
                        head_turn(l, s - 2)
                    if 1 <= s <= HEADS:
                        head_scores(l, s - 1)
                    if s < HEADS:
                        head_qk(l, s)
                for i in range(index["WO0", 0], index["MV1", 3] + 1):
                    gemm(l, i)
                turn_x(l, "XT0b", 0, 1)
                turn_x(l, "XT1b", 1, 2)
                ready(l, "XT0b")
                ready(l, "XT1b")
                for j in range(4):
                    gemm(l, index["XQ0", j])
                ready(l, "XQ0")
                ready(l, "MK1")
                for s in range(X_H + 2):
                    if s == 2:
                        ready(l, "XQ1")
                        ready(l, "MV1")
                    if s < X_H:
                        head_scores(l, HEADS + s)
                    if 1 <= s <= X_H:
                        head_turn(l, HEADS + s - 1)
                    for i in xturns[s]:
                        gemm(l, i)
                    if s >= 2:
                        head_values(l, HEADS + s - 2)
                for i in range(index["XO0", 3], index["XO1", 3] + 1):
                    gemm(l, i)
                turn_x(l, "XT0c", 0, 3)
                turn_x(l, "XT1c", 1, 4)
                ready(l, "XT0c")
                ready(l, "XT1c")
                open_job(l, "RT")
                for j in range(2):
                    parts = sub_in(l, index["RT", j])
                    for k in range(4):
                        kc = 4 * j + k
                        lhs = tuple(v[:, k * NE:k * NE + P] for v in parts)
                        ins = product(banks("RT")[0][:, 0:T], lhs, tuple(v[:, kc, :] for v in xT), kc == 0, kc == KC - 1)
                    ins.then_inc(split_free.sem, 1)
                open_job(l, "GT")
                ready(l, "RT")
                pe.nop().then_inc(paused_t, 1)
                for t in range(TT):
                    ins = nc.tensor.transpose(banks("GT")[0][:, t * NE:(t + 1) * NE], logitT[0:NE, t * P:(t + 1) * P],
                                              ident[0:NE, 0:NE])
                ins.then_inc(turned.sem, 1)
                ready(l, "GT")
                gather(l)
                experts_up(l, N1, 0, range(4), None, 0)
                turn_sel(l)
                expert_turn(l, 0, 0, N1 + 4, None, lambda: place_gates(l))
                with pe.Fori(0, TURNS) as p:
                    for j in range(1, EPG + 1):
                        expert_turn(l, p * EPG + j, j % EPG, 6 * (j - 1), p)
                for j in range(2):
                    expert_turn(l, NE - 3 + j, 1 + j, NSUB - N_EPI + 6 * j)
                turn_a(l, NE - 1, 1)
                experts_down(l, NE - 1, NSUB - 2, 1, False, True)
                for g in range(NG):
                    scatter(l, g)
                over = overflow(pe, l, paused_t)
                with pe.If(over > 0):
                    further_tokens(l)
                with pe.If(over < 1):
                    for s_, n in ((ov_gathered, 1), (ov_upped, EPG), (ov_turned, EPG), (ov_used, EPG), (summed, 1)):
                        pe.nop().then_inc(s_.sem, n)


_INS = ["x", "mem", "positions", "w_in", "b_forget", "mla_q_gain", "mla_kv_gain", "mla_w_uq", "mla_w_ukv",
        "w_mix_out", "ln_mix_g", "ln_mix_b", "xattn_w_q", "xattn_w_kv", "xattn_w_o", "ln_mem_g", "ln_mem_b",
        "router_w", "router_bias", "expert_w_gate", "expert_w_up", "expert_w_down", "ln_ffn_g", "ln_ffn_b"]


def kernel(**inputs):
    import concourse.bacc as _bacc
    from concourse.bass_utils import run_bass_kernel_spmd as _run

    nc = _bacc.Bacc("TRN2", target_bir_lowering=False, num_devices=1)
    arrays, args = {}, []
    for name in _INS:
        a = np.ascontiguousarray(inputs[name])
        arrays[f"in_{name}_dram"] = a
        args.append(nc.dram_tensor(f"in_{name}_dram", a.shape, mybir.dt.from_np(a.dtype), kind="ExternalInput").ap())
    out = nc.dram_tensor("out_dram", inputs["x"].shape, F32, kind="ExternalOutput").ap()
    build(nc, *args, out)
    r = _run(nc, [arrays], core_ids=[0])
    return r.results[0]["out_dram"]
```
